# Optimizing a Trainium2 kernel written in Bass

```python
import jax, jax.numpy as jnp
from jax import lax
import numpy as np
import math
import jax
import jax.numpy as jnp

D_MODEL = 1024
BATCH = 1
SEQ = 512
DEPTH = 2

CHUNK = 64
QBLOCK = 128
HEAD_DIM = 64
EPS = 1e-6
H_FOX = 8
H_CHK = 8
N_LEFT_CHUNKS = 8
BAND = (N_LEFT_CHUNKS + 1) * CHUNK
REL_CLIP = 256
N_REL = CHUNK - 1 + REL_CLIP + 1
FORGET_BIAS = 3.0
H_SB = 8
H_MLA = 8
Q_LORA = 384
KV_LORA = 256
NOPE_DIM = 64
ROPE_DIM = 32
V_DIM = 64
ROPE_THETA = 10000.0
D_FF = 4 * D_MODEL
N_EVEN = (DEPTH + 1) // 2
N_ODD = DEPTH // 2

W_FOX = H_FOX * HEAD_DIM
W_CHK = H_CHK * HEAD_DIM
W_SB = H_SB * HEAD_DIM
W_MLA = H_MLA * V_DIM
SPLIT_AB = [W_FOX, W_FOX, W_FOX, H_FOX, W_CHK, W_CHK, W_CHK]
SPLIT_CD = [W_SB, W_SB, W_SB, Q_LORA, KV_LORA, ROPE_DIM]
IN_AB = sum(SPLIT_AB)
IN_CD = sum(SPLIT_CD)
MIX_AB = W_FOX + W_CHK
MIX_CD = W_SB + W_MLA


def _split(h, sizes):
    return jnp.split(h, np.cumsum(sizes)[:-1].tolist(), axis=-1)

def rmsnorm(x, g):
    xf = x.astype(jnp.float32)
    y = xf * lax.rsqrt(jnp.mean(xf * xf, axis=-1, keepdims=True) + EPS)
    return (y * g.astype(jnp.float32)).astype(x.dtype)

def rope(x, positions):
    half = ROPE_DIM // 2
    inv_freq = ROPE_THETA ** (-jnp.arange(half, dtype=jnp.float32) / half)
    ang = positions.astype(jnp.float32)[..., None] * inv_freq
    cos = jnp.cos(ang)[:, :, None, :]
    sin = jnp.sin(ang)[:, :, None, :]
    x1 = x[..., :half].astype(jnp.float32)
    x2 = x[..., half:].astype(jnp.float32)
    out = jnp.concatenate([x1 * cos - x2 * sin, x2 * cos + x1 * sin], axis=-1)
    return out.astype(x.dtype)

def _sweep_query_blocks(block_fn, seq):
    out = lax.map(block_fn, jnp.arange(seq // QBLOCK))
    nb, b, qb, h, dv = out.shape
    return jnp.moveaxis(out, 0, 1).reshape(b, nb * qb, h, dv)

def fox_attention(q, k, v, log_f):
    seq = q.shape[1]
    scale = HEAD_DIM ** -0.5
    cum = jnp.transpose(jnp.cumsum(log_f, axis=1), (0, 2, 1))
    k_pos = jnp.arange(seq)

    def block(i):
        start = i * QBLOCK
        qb = lax.dynamic_slice_in_dim(q, start, QBLOCK, axis=1)
        cq = lax.dynamic_slice_in_dim(cum, start, QBLOCK, axis=2)
        q_pos = start + jnp.arange(QBLOCK)
        s = jnp.einsum('bqhd,bkhd->bhqk', qb, k).astype(jnp.float32) * scale
        s = s + cq[..., :, None] - cum[..., None, :]
        mask = k_pos[None, :] <= q_pos[:, None]
        p = jax.nn.softmax(jnp.where(mask, s, -jnp.inf), axis=-1)
        return jnp.einsum('bhqk,bkhd->bqhd', p.astype(v.dtype), v)

    return _sweep_query_blocks(block, seq)

def chunked_relpos_attention(q, k, v, rel_bias):
    b, seq, h, d = q.shape
    nc = seq // CHUNK
    left = N_LEFT_CHUNKS * CHUNK
    scale = HEAD_DIM ** -0.5

    def band(t):
        tp = jnp.pad(t, ((0, 0), (left, 0), (0, 0), (0, 0)))
        tp = tp.reshape(b, nc + N_LEFT_CHUNKS, CHUNK, h, d)
        return jnp.concatenate([tp[:, i:i + nc] for i in range(N_LEFT_CHUNKS + 1)], axis=2)

    kb, vb = band(k), band(v)
    qc = q.reshape(b, nc, CHUNK, h, d)
    rel = np.arange(CHUNK)[:, None] + left - np.arange(BAND)[None, :]
    rel_idx = np.clip(rel, -(CHUNK - 1), REL_CLIP) + (CHUNK - 1)
    bias = rel_bias[:, rel_idx].astype(jnp.float32)
    s = jnp.einsum('bcqhd,bckhd->bhcqk', qc, kb).astype(jnp.float32) * scale
    s = s + bias[None, :, None]
    key_abs = jnp.arange(nc)[:, None] * CHUNK - left + jnp.arange(BAND)[None, :]
    valid = (key_abs >= 0)[None, None, :, None, :]
    p = jax.nn.softmax(jnp.where(valid, s, -jnp.inf), axis=-1)
    out = jnp.einsum('bhcqk,bckhd->bcqhd', p.astype(v.dtype), vb)
    return out.reshape(b, seq, h, d)

def stick_breaking_attention(q, k, v):
    seq = q.shape[1]
    scale = HEAD_DIM ** -0.5
    k_pos = jnp.arange(seq)

    def block(i):
        start = i * QBLOCK
        qb = lax.dynamic_slice_in_dim(q, start, QBLOCK, axis=1)
        q_pos = start + jnp.arange(QBLOCK)
        z = jnp.einsum('bqhd,bkhd->bhqk', qb, k).astype(jnp.float32) * scale
        mask = k_pos[None, :] < q_pos[:, None]
        log_beta = jax.nn.log_sigmoid(z)
        log_keep = jnp.where(mask, jax.nn.log_sigmoid(-z), 0.0)
        suffix = lax.cumsum(log_keep, axis=3, reverse=True) - log_keep
        a = jnp.where(mask, jnp.exp(log_beta + suffix), 0.0)
        return jnp.einsum('bhqk,bkhd->bqhd', a.astype(v.dtype), v)

    return _sweep_query_blocks(block, seq)

def mla_attention(q_nope, q_rope, k_nope, k_rope, v):
    seq = q_nope.shape[1]
    scale = (NOPE_DIM + ROPE_DIM) ** -0.5
    k_chunk = jnp.arange(seq) // CHUNK

    def block(i):
        start = i * QBLOCK
        qn = lax.dynamic_slice_in_dim(q_nope, start, QBLOCK, axis=1)
        qr = lax.dynamic_slice_in_dim(q_rope, start, QBLOCK, axis=1)
        q_chunk = (start + jnp.arange(QBLOCK)) // CHUNK
        s = (jnp.einsum('bqhd,bkhd->bhqk', qn, k_nope)
             + jnp.einsum('bqhr,bkr->bhqk', qr, k_rope)).astype(jnp.float32) * scale
        mask = k_chunk[None, :] <= q_chunk[:, None]
        p = jax.nn.softmax(jnp.where(mask, s, -jnp.inf), axis=-1)
        return jnp.einsum('bhqk,bkhd->bqhd', p.astype(v.dtype), v)

    return _sweep_query_blocks(block, seq)

def even_mixer(h, w_in, b_forget, rel_bias, w_out):
    b, s, _ = h.shape
    qa, ka, va, fa, qb, kb, vb = _split(h @ w_in, SPLIT_AB)
    heads = lambda t, n: t.reshape(b, s, n, HEAD_DIM)
    log_f = jax.nn.log_sigmoid((fa + b_forget).astype(jnp.float32))
    o_a = fox_attention(heads(qa, H_FOX), heads(ka, H_FOX), heads(va, H_FOX), log_f)
    o_b = chunked_relpos_attention(heads(qb, H_CHK), heads(kb, H_CHK), heads(vb, H_CHK), rel_bias)
    o = jnp.concatenate([o_a.reshape(b, s, W_FOX), o_b.reshape(b, s, W_CHK)], axis=-1)
    return o @ w_out

def odd_mixer(h, positions, w_in, q_norm, kv_norm, w_uq, w_ukv, w_out):
    b, s, _ = h.shape
    qc, kc, vc, c_q, c_kv, k_r = _split(h @ w_in, SPLIT_CD)
    heads = lambda t, n, d: t.reshape(b, s, n, d)
    o_c = stick_breaking_attention(heads(qc, H_SB, HEAD_DIM), heads(kc, H_SB, HEAD_DIM), heads(vc, H_SB, HEAD_DIM))
    q_full = heads(rmsnorm(c_q, q_norm) @ w_uq, H_MLA, NOPE_DIM + ROPE_DIM)
    q_nope, q_rope = q_full[..., :NOPE_DIM], rope(q_full[..., NOPE_DIM:], positions)
    kv_full = heads(rmsnorm(c_kv, kv_norm) @ w_ukv, H_MLA, NOPE_DIM + V_DIM)
    k_nope, v_d = kv_full[..., :NOPE_DIM], kv_full[..., NOPE_DIM:]
    k_rope = rope(k_r[:, :, None, :], positions)[:, :, 0, :]
    o_d = mla_attention(q_nope, q_rope, k_nope, k_rope, v_d)
    o = jnp.concatenate([o_c.reshape(b, s, W_SB), o_d.reshape(b, s, W_MLA)], axis=-1)
    return o @ w_out

def squared_relu_mlp(h, w_up, w_down):
    return jnp.square(jax.nn.relu(h @ w_up)) @ w_down

def first_inputs(seed: int = 0) -> dict:
    key = jax.random.key(seed)
    ks = jax.random.split(key, 20)
    nrm = lambda k, shape, fan_in: jax.random.normal(k, shape, jnp.float32) * fan_in ** -0.5
    gain = lambda k, shape: 1.0 + 0.05 * jax.random.normal(k, shape, jnp.float32)
    x = jax.random.normal(ks[0], (BATCH, SEQ, D_MODEL), jnp.float32)
    offset = jax.random.randint(ks[1], (BATCH, 1), 0, 100000, dtype=jnp.int32)
    positions = offset + jnp.arange(SEQ, dtype=jnp.int32)[None, :]
    return {
        "x": x,
        "positions": positions,
        "norm_mix": gain(ks[2], (DEPTH, D_MODEL)),
        "norm_mlp": gain(ks[3], (DEPTH, D_MODEL)),
        "norm_final": gain(ks[4], (D_MODEL,)),
        "w_in_ab": nrm(ks[5], (N_EVEN, D_MODEL, IN_AB), D_MODEL),
        "b_forget": FORGET_BIAS + 0.5 * jax.random.normal(ks[6], (N_EVEN, H_FOX), jnp.float32),
        "rel_bias": 0.2 * jax.random.normal(ks[7], (N_EVEN, H_CHK, N_REL), jnp.float32),
        "w_out_ab": nrm(ks[8], (N_EVEN, MIX_AB, D_MODEL), MIX_AB),
        "w_in_cd": nrm(ks[9], (N_ODD, D_MODEL, IN_CD), D_MODEL),
        "q_norm": gain(ks[10], (N_ODD, Q_LORA)),
        "kv_norm": gain(ks[11], (N_ODD, KV_LORA)),
        "w_uq": nrm(ks[12], (N_ODD, Q_LORA, H_MLA * (NOPE_DIM + ROPE_DIM)), Q_LORA),
        "w_ukv": nrm(ks[13], (N_ODD, KV_LORA, H_MLA * (NOPE_DIM + V_DIM)), KV_LORA),
        "w_out_cd": nrm(ks[14], (N_ODD, MIX_CD, D_MODEL), MIX_CD),
        "w_up": nrm(ks[15], (DEPTH, D_MODEL, D_FF), D_MODEL),
        "w_down": nrm(ks[16], (DEPTH, D_FF, D_MODEL), D_FF),
    }

def first_block(x, positions, norm_mix, norm_mlp, norm_final, w_in_ab, b_forget, rel_bias, w_out_ab,
              w_in_cd, q_norm, kv_norm, w_uq, w_ukv, w_out_cd, w_up, w_down):
    for layer in range(DEPTH):
        h = rmsnorm(x, norm_mix[layer])
        if layer % 2 == 0:
            e = layer // 2
            x = x + even_mixer(h, w_in_ab[e], b_forget[e], rel_bias[e], w_out_ab[e])
        else:
            o = layer // 2
            x = x + odd_mixer(h, positions, w_in_cd[o], q_norm[o], kv_norm[o], w_uq[o], w_ukv[o], w_out_cd[o])
        x = x + squared_relu_mlp(rmsnorm(x, norm_mlp[layer]), w_up[layer], w_down[layer])
    return rmsnorm(x, norm_final)


DEPTH_2 = 1

NORM_EPS = 1e-6
NEG_INF = -1e30
FORCE_SCORE = 1e9

DIFF_HEADS = 4
DIFF_VDIM = 2 * HEAD_DIM
DIFF_Q_BLOCK = 128

NSA_HEADS = 8
NSA_KV_GROUPS = 2
NSA_HPG = NSA_HEADS // NSA_KV_GROUPS
CMP_LEN = 32
CMP_STRIDE = 16
CMP_HIDDEN = 4 * HEAD_DIM
SEL_LEN = 64
SEL_TOPK = 16
WINDOW = 512
NSA_Q_BLOCK = 64

D_FF_2 = int(math.ceil(8 * D_MODEL / 3 / 256)) * 256

DIFF_QK = DIFF_HEADS * 2 * HEAD_DIM
DIFF_V = DIFF_HEADS * DIFF_VDIM
NSA_Q = NSA_HEADS * HEAD_DIM
NSA_KV = NSA_KV_GROUPS * HEAD_DIM
NSA_GATES = 3 * NSA_HEADS
MERGE_GATES = 2 * D_MODEL
IN_SPLITS = (DIFF_QK, DIFF_QK, DIFF_V, NSA_Q, NSA_KV, NSA_KV, NSA_KV, NSA_KV, NSA_KV, NSA_KV, NSA_GATES, MERGE_GATES)
IN_DIM = sum(IN_SPLITS)
A_WIDTH = DIFF_V
B_WIDTH = NSA_HEADS * HEAD_DIM


def lambda_init(layer):
    return 0.8 - 0.6 * math.exp(-0.3 * layer)

def rms_norm(x, g):
    xf = x.astype(jnp.float32)
    y = xf * lax.rsqrt(jnp.mean(xf * xf, axis=-1, keepdims=True) + NORM_EPS)
    return (y * g.astype(jnp.float32)).astype(x.dtype)

def rope_tables(positions, dim):
    inv_freq = 1.0 / (ROPE_THETA ** (jnp.arange(0, dim, 2, dtype=jnp.float32) / dim))
    ang = positions.astype(jnp.float32)[..., None] * inv_freq
    return jnp.cos(ang), jnp.sin(ang)

def apply_rope(x, cos, sin):
    half = x.shape[-1] // 2
    xf = x.astype(jnp.float32)
    x1, x2 = xf[..., :half], xf[..., half:]
    return jnp.concatenate([x1 * cos - x2 * sin, x2 * cos + x1 * sin], axis=-1).astype(x.dtype)

def differential_attention(q, k, v, lam):
    B, S, H, _, dh = q.shape
    nblk = S // DIFF_Q_BLOCK
    scale = dh ** -0.5
    kpos = jnp.arange(S)

    def one_block(i):
        s0 = i * DIFF_Q_BLOCK
        qb = lax.dynamic_slice_in_dim(q, s0, DIFF_Q_BLOCK, axis=1)
        s = jnp.einsum('bqhcd,bkhcd->bhcqk', qb, k).astype(jnp.float32) * scale
        qpos = s0 + jnp.arange(DIFF_Q_BLOCK)
        causal = kpos[None, :] <= qpos[:, None]
        p = jax.nn.softmax(jnp.where(causal, s, NEG_INF), axis=-1)
        a = p[:, :, 0] - lam * p[:, :, 1]
        return jnp.einsum('bhqk,bkhe->bqhe', a.astype(v.dtype), v)

    o = lax.map(one_block, jnp.arange(nblk))
    return o.transpose(1, 0, 2, 3, 4).reshape(B, S, H, v.shape[-1])

def compress(x, pe, w1, w2):
    B, S, G, dh = x.shape
    nc = (S - CMP_LEN) // CMP_STRIDE + 1
    idx = np.arange(nc)[:, None] * CMP_STRIDE + np.arange(CMP_LEN)[None, :]
    blk = x[:, idx] + pe[None, None, :, None, :]
    blk = blk.transpose(0, 1, 3, 2, 4).reshape(B, nc, G, CMP_LEN * dh)
    return jax.nn.silu(blk @ w1) @ w2

def nsa_attention(q, kc, vc, ks, vs, kw, vw):
    B, S, G, hpg, dh = q.shape
    nc = kc.shape[1]
    nsb = S // SEL_LEN
    topk = min(SEL_TOPK, nsb)
    nblk = S // NSA_Q_BLOCK
    scale = dh ** -0.5
    cmp_end = np.arange(nc) * CMP_STRIDE + CMP_LEN - 1
    ci = np.arange(nc)[:, None] * CMP_STRIDE
    sj = np.arange(nsb)[None, :] * SEL_LEN
    overlap = jnp.asarray(((ci < sj + SEL_LEN) & (ci + CMP_LEN > sj)).astype(np.float32))
    kb = ks.reshape(B, nsb, SEL_LEN, G, dh).transpose(0, 3, 1, 2, 4)
    vb = vs.reshape(B, nsb, SEL_LEN, G, dh).transpose(0, 3, 1, 2, 4)
    kw_pad = jnp.pad(kw, ((0, 0), (WINDOW, 0), (0, 0), (0, 0)))
    vw_pad = jnp.pad(vw, ((0, 0), (WINDOW, 0), (0, 0), (0, 0)))
    b_idx = jnp.arange(B)[:, None, None, None]
    g_idx = jnp.arange(G)[None, None, :, None]
    blk_ids = jnp.arange(nsb)
    sel_off = jnp.arange(SEL_LEN)

    def one_block(i):
        s0 = i * NSA_Q_BLOCK
        qpos = s0 + jnp.arange(NSA_Q_BLOCK)
        qb = lax.dynamic_slice_in_dim(q, s0, NSA_Q_BLOCK, axis=1)
        sc = jnp.einsum('bqghd,bcgd->bqghc', qb, kc).astype(jnp.float32) * scale
        cm = (cmp_end[None, :] <= qpos[:, None])[None, :, None, None, :]
        pc = jax.nn.softmax(jnp.where(cm, sc, NEG_INF), axis=-1) * cm
        o_c = jnp.einsum('bqghc,bcgd->bqghd', pc.astype(vc.dtype), vc)
        imp = jnp.einsum('bqgc,cn->bqgn', pc.sum(axis=3), overlap)
        qblk = qpos // SEL_LEN
        forced = (blk_ids[None, :] == 0) | (blk_ids[None, :] == qblk[:, None]) | (blk_ids[None, :] == qblk[:, None] - 1)
        causal_blk = blk_ids[None, :] <= qblk[:, None]
        imp = jnp.where(forced[None, :, None, :], FORCE_SCORE, imp)
        imp = jnp.where(causal_blk[None, :, None, :], imp, NEG_INF)
        _, idx = lax.top_k(imp, topk)
        ksel = kb[b_idx, g_idx, idx]
        vsel = vb[b_idx, g_idx, idx]
        ss = jnp.einsum('bqghd,bqgnld->bqghnl', qb, ksel).astype(jnp.float32) * scale
        kp = idx[..., None] * SEL_LEN + sel_off
        smask = (kp <= qpos[None, :, None, None, None])[:, :, :, None]
        ss = jnp.where(smask, ss, NEG_INF).reshape(B, NSA_Q_BLOCK, G, hpg, topk * SEL_LEN)
        ps = jax.nn.softmax(ss, axis=-1).reshape(B, NSA_Q_BLOCK, G, hpg, topk, SEL_LEN)
        o_s = jnp.einsum('bqghnl,bqgnld->bqghd', ps.astype(vsel.dtype), vsel)
        kwb = lax.dynamic_slice_in_dim(kw_pad, s0, NSA_Q_BLOCK + WINDOW, axis=1)
        vwb = lax.dynamic_slice_in_dim(vw_pad, s0, NSA_Q_BLOCK + WINDOW, axis=1)
        kpos = s0 - WINDOW + jnp.arange(NSA_Q_BLOCK + WINDOW)
        dist = qpos[:, None] - kpos[None, :]
        wmask = ((dist >= 0) & (dist < WINDOW) & (kpos[None, :] >= 0))[None, :, None, None, :]
        sw = jnp.einsum('bqghd,bkgd->bqghk', qb, kwb).astype(jnp.float32) * scale
        pw = jax.nn.softmax(jnp.where(wmask, sw, NEG_INF), axis=-1)
        o_w = jnp.einsum('bqghk,bkgd->bqghd', pw.astype(vwb.dtype), vwb)
        return o_c, o_s, o_w

    o_c, o_s, o_w = lax.map(one_block, jnp.arange(nblk))

    def to_seq(o):
        return o.transpose(1, 0, 2, 3, 4, 5).reshape(B, S, G * hpg, dh)

    return to_seq(o_c), to_seq(o_s), to_seq(o_w)

def hybrid_mixer(u, cos, sin, layer, w_in, diff_lambda, diff_subln_g, cmp_pe_k, cmp_pe_v,
                 cmp_k_w1, cmp_k_w2, cmp_v_w1, cmp_v_w2, w_branch_a, w_branch_b, w_out):
    B, S, _ = u.shape
    G, dh = NSA_KV_GROUPS, HEAD_DIM
    split_at = np.cumsum(IN_SPLITS)[:-1].tolist()
    (dq, dk, dv, nq, kc_, vc_, ks_, vs_, kw_, vw_, ngate, mgate) = jnp.split(u @ w_in, split_at, axis=-1)
    c4, s4 = cos[:, :, None, None, :], sin[:, :, None, None, :]
    c3, s3 = cos[:, :, None, :], sin[:, :, None, :]
    dq = apply_rope(dq.reshape(B, S, DIFF_HEADS, 2, dh), c4, s4)
    dk = apply_rope(dk.reshape(B, S, DIFF_HEADS, 2, dh), c4, s4)
    dv = dv.reshape(B, S, DIFF_HEADS, DIFF_VDIM)
    lam_init = lambda_init(layer)
    lf = diff_lambda.astype(jnp.float32)
    lam = jnp.exp(jnp.sum(lf[0] * lf[1])) - jnp.exp(jnp.sum(lf[2] * lf[3])) + lam_init
    y_a = differential_attention(dq, dk, dv, lam)
    y_a = rms_norm(y_a, diff_subln_g) * (1.0 - lam_init)
    y_a = y_a.reshape(B, S, A_WIDTH) @ w_branch_a
    nq = apply_rope(nq.reshape(B, S, NSA_HEADS, dh), c3, s3).reshape(B, S, G, NSA_HPG, dh)

    def kv(t):
        return t.reshape(B, S, G, dh)

    k_cmp = compress(apply_rope(kv(kc_), c3, s3), cmp_pe_k, cmp_k_w1, cmp_k_w2)
    v_cmp = compress(kv(vc_), cmp_pe_v, cmp_v_w1, cmp_v_w2)
    k_sel = apply_rope(kv(ks_), c3, s3)
    k_win = apply_rope(kv(kw_), c3, s3)
    o_c, o_s, o_w = nsa_attention(nq, k_cmp, v_cmp, k_sel, kv(vs_), k_win, kv(vw_))
    g = jax.nn.sigmoid(ngate.astype(jnp.float32)).reshape(B, S, 3, NSA_HEADS, 1).astype(u.dtype)
    y_b = g[:, :, 0] * o_c + g[:, :, 1] * o_s + g[:, :, 2] * o_w
    y_b = y_b.reshape(B, S, B_WIDTH) @ w_branch_b
    mg = jax.nn.sigmoid(mgate.astype(jnp.float32)).reshape(B, S, 2, D_MODEL).astype(u.dtype)
    return (mg[:, :, 0] * y_a + mg[:, :, 1] * y_b) @ w_out

def swiglu(u, w_gate, w_up, w_down):
    return (jax.nn.silu(u @ w_gate) * (u @ w_up)) @ w_down

def second_inputs(seed: int = 0) -> dict:
    key = jax.random.key(seed)
    ks = jax.random.split(key, 22)

    def nrm(k, shape, scale):
        return jax.random.normal(k, shape, jnp.float32) * scale

    return {
        "x": nrm(ks[0], (BATCH, SEQ, D_MODEL), 1.0),
        "positions": jnp.tile(jnp.arange(SEQ, dtype=jnp.int32)[None, :], (BATCH, 1)),
        "attn_norm_g": 1.0 + nrm(ks[1], (DEPTH_2, D_MODEL), 0.02),
        "w_in": nrm(ks[2], (DEPTH_2, D_MODEL, IN_DIM), D_MODEL ** -0.5),
        "diff_lambda": nrm(ks[3], (DEPTH_2, 4, HEAD_DIM), 0.1),
        "diff_subln_g": 1.0 + nrm(ks[4], (DEPTH_2, DIFF_VDIM), 0.02),
        "cmp_pe_k": nrm(ks[5], (DEPTH_2, CMP_LEN, HEAD_DIM), 0.1),
        "cmp_pe_v": nrm(ks[6], (DEPTH_2, CMP_LEN, HEAD_DIM), 0.1),
        "cmp_k_w1": nrm(ks[7], (DEPTH_2, CMP_LEN * HEAD_DIM, CMP_HIDDEN), (CMP_LEN * HEAD_DIM) ** -0.5),
        "cmp_k_w2": nrm(ks[8], (DEPTH_2, CMP_HIDDEN, HEAD_DIM), CMP_HIDDEN ** -0.5),
        "cmp_v_w1": nrm(ks[9], (DEPTH_2, CMP_LEN * HEAD_DIM, CMP_HIDDEN), (CMP_LEN * HEAD_DIM) ** -0.5),
        "cmp_v_w2": nrm(ks[10], (DEPTH_2, CMP_HIDDEN, HEAD_DIM), CMP_HIDDEN ** -0.5),
        "w_branch_a": nrm(ks[11], (DEPTH_2, A_WIDTH, D_MODEL), A_WIDTH ** -0.5),
        "w_branch_b": nrm(ks[12], (DEPTH_2, B_WIDTH, D_MODEL), B_WIDTH ** -0.5),
        "w_out": nrm(ks[13], (DEPTH_2, D_MODEL, D_MODEL), D_MODEL ** -0.5),
        "ffn_norm_g": 1.0 + nrm(ks[14], (DEPTH_2, D_MODEL), 0.02),
        "w_gate": nrm(ks[15], (DEPTH_2, D_MODEL, D_FF_2), D_MODEL ** -0.5),
        "w_up": nrm(ks[16], (DEPTH_2, D_MODEL, D_FF_2), D_MODEL ** -0.5),
        "w_down": nrm(ks[17], (DEPTH_2, D_FF_2, D_MODEL), D_FF_2 ** -0.5),
        "final_norm_g": 1.0 + nrm(ks[18], (D_MODEL,), 0.02),
    }

def second_block(x, positions, attn_norm_g, w_in, diff_lambda, diff_subln_g, cmp_pe_k, cmp_pe_v,
              cmp_k_w1, cmp_k_w2, cmp_v_w1, cmp_v_w2, w_branch_a, w_branch_b, w_out,
              ffn_norm_g, w_gate, w_up, w_down, final_norm_g):
    cos, sin = rope_tables(positions, HEAD_DIM)
    h = x
    for layer in range(DEPTH_2):
        u = rms_norm(h, attn_norm_g[layer])
        h = h + hybrid_mixer(u, cos, sin, layer, w_in[layer], diff_lambda[layer], diff_subln_g[layer],
                             cmp_pe_k[layer], cmp_pe_v[layer], cmp_k_w1[layer], cmp_k_w2[layer],
                             cmp_v_w1[layer], cmp_v_w2[layer], w_branch_a[layer], w_branch_b[layer],
                             w_out[layer])
        u = rms_norm(h, ffn_norm_g[layer])
        h = h + swiglu(u, w_gate[layer], w_up[layer], w_down[layer])
    return rms_norm(h, final_norm_g)


def setup_inputs(seed=0):
    out = dict(first_inputs(seed))
    for name, value in second_inputs(seed + 1).items():
        if name != "x":
            out[name + "_2"] = value
    return out


def reference(
    x, positions, norm_mix, norm_mlp, norm_final, w_in_ab, b_forget, rel_bias, w_out_ab,
    w_in_cd, q_norm, kv_norm, w_uq, w_ukv, w_out_cd, w_up, w_down, positions_2, attn_norm_g_2,
    w_in_2, diff_lambda_2, diff_subln_g_2, cmp_pe_k_2, cmp_pe_v_2, cmp_k_w1_2, cmp_k_w2_2,
    cmp_v_w1_2, cmp_v_w2_2, w_branch_a_2, w_branch_b_2, w_out_2, ffn_norm_g_2, w_gate_2, w_up_2,
    w_down_2, final_norm_g_2,
):
    x = first_block(
        x, positions, norm_mix, norm_mlp, norm_final, w_in_ab, b_forget, rel_bias, w_out_ab,
        w_in_cd, q_norm, kv_norm, w_uq, w_ukv, w_out_cd, w_up, w_down,
    )
    return second_block(
        x, positions_2, attn_norm_g_2, w_in_2, diff_lambda_2, diff_subln_g_2, cmp_pe_k_2,
        cmp_pe_v_2, cmp_k_w1_2, cmp_k_w2_2, cmp_v_w1_2, cmp_v_w2_2, w_branch_a_2, w_branch_b_2,
        w_out_2, ffn_norm_g_2, w_gate_2, w_up_2, w_down_2, final_norm_g_2,
    )


_drawn_inputs = setup_inputs


def setup_inputs(seed=0):
    import zlib

    import numpy as np

    out = dict(_drawn_inputs(seed))
    spreads = {}
    factors = {'rel_bias': 2.786,
     'q_norm': 8.0,
     'kv_norm': 5.384,
     'attn_norm_g_2': 4.949,
     'diff_subln_g_2': 7.46,
     'cmp_pe_k_2': 8.0,
     'cmp_pe_v_2': 3.51,
     'ffn_norm_g_2': 4.114,
     'final_norm_g_2': 2.808}
    for name, (base, spread) in spreads.items():
        noise = np.random.default_rng([zlib.crc32(name.encode()), seed]).standard_normal(out[name].shape)
        drawn = base * np.exp(spread * noise) if base else spread * noise
        out[name] = jnp.asarray(drawn.astype(out[name].dtype))
    for name, factor in factors.items():
        out[name] = (out[name] * factor).astype(out[name].dtype)
    return out
```

```python
from contextlib import ExitStack, contextmanager

import numpy as np

import concourse.bass as bass
from concourse import mybir

F32 = mybir.dt.float32
F32R = mybir.dt.float32r
I32 = mybir.dt.int32
ALU = mybir.AluOpType
ACT = mybir.ActivationFunctionType
X = mybir.AxisListType.X

P = 128
S = 512
D = 1024
KT = D // P
NB = S // P
SLAB = 8 * P
HEAD = 64
CHUNK = 64
EPS = 1e-6
NEG = -1e30
Q_TILES, KV_TILES = 3, 2
C_TILES = Q_TILES + KV_TILES
MLA_SCALE = 96 ** -0.5
QK_SCALE = HEAD ** -0.5
LAM_INIT = 0.8 - 0.6
FF2_TILES = 22
N_REL = 320
E_LEN = 640
CMP_BLOCKS, CMP_STRIDE, CMP_LEN, CMP_M = 31, 16, 32, 16
CC = 2 * CMP_BLOCKS
TWO_PI = 2 * np.pi
PI_PARTS = [6.25, 0.033203125, -1.811981201171875e-05]
PI_PARTS.append(TWO_PI - sum(PI_PARTS))
ROUND = 1.5 * 2 ** 23

PARAM_COLS = [("mix0", 8), ("mlp0", 8), ("mix1", 8), ("mlp1", 8), ("final1", 8), ("q_norm", 3),
              ("kv_norm", 2), ("attn2", 8), ("ffn2", 8), ("final2", 8), ("subln", 1), ("b_forget", 1),
              ("pe_k", 16), ("pe_v", 16), ("w2_k", 128), ("w2_v", 128)]
CONST_COLS = [("ident", 128), ("anti", 128), ("causal", 128), ("strict", 128), ("chunk", 128),
              ("ones", 128), ("onehot", 8), ("freq1", 1), ("sign1", 1), ("freq2", 1), ("sign2", 1),
              ("half_pi", 1), ("cmp_neg", NB * CMP_BLOCKS), ("cmp_keep", NB * CMP_BLOCKS)]


def columns(spec):
    at, out = 0, {}
    for name, width in spec:
        out[name] = slice(at, at + width)
        at += width
    return out, at


PC, N_PARAM = columns(PARAM_COLS)
CO, N_CONST = columns(CONST_COLS)


class Count:

    def __init__(self):
        self.now, self.loops = 0, []

    def at(self, off=0, scale=1):
        value = self.now * scale + off
        for i, per in self.loops:
            value = i * (per * scale) + value
        return value

    def past(self, least):
        return self.now > least

    @property
    def slot(self):
        return self.now % 2


class Counts:
    NAMES = ("slab", "gemm", "step", "out", "hi", "lo", "h32", "acc", "rstd", "rope", "ln", "link")

    def __init__(self):
        counts = [Count() for name in self.NAMES]
        (self.slab, self.gemm, self.step, self.out, self.hi, self.lo, self.h32, self.acc, self.rstd,
         self.rope, self.ln, self.link) = counts
        self.named = dict(zip(self.NAMES, counts))

    @contextmanager
    def loop(self, eng, times, **per):
        with eng.Fori(0, times) as i:
            start = {name: self.named[name].now for name in per}
            before = {name: self.named[name].now for name in self.NAMES}
            for name, by in per.items():
                self.named[name].loops.append((i, by))
            yield i
            for name in self.NAMES:
                made = self.named[name].now - before[name]
                assert made == per.get(name, 0), f"{name}: the body makes {made}, said {per.get(name, 0)}"
            for name in per:
                self.named[name].loops.pop()
        for name, by in per.items():
            self.named[name].now = start[name] + times * by


PLAIN = [("v", 8, 1), ("q", 8, 1), ("vt", 0, 0), ("k", 8, 1)]
ROPED = [("q", 8, 1), ("k", 8, 1), ("v", 8, 1), ("vt", 0, 0)]
LATENT = [("q0", 3, 0), ("kv0", 2, 1), ("q1", 3, 0), ("kv1", 2, 1), ("vt", 0, 0)]
QUERY = [("q", 8, 1)]


def work(proj, slot, slots):
    total = sum(n for _, n, _ in proj)
    low, high = total * slot // slots, total * (slot + 1) // slots
    at = 0
    for name, n, ends in proj:
        if n == 0:
            if low < at <= high or (at == 0 and slot == 0):
                yield name, 0, 0, 0
        for j in range(n):
            if low <= at < high:
                yield name, j, n, ends and j == n - 1
            at += 1


def build(nc, slabs, x_in, params_in, consts_in, pos1_in, pos2_in, rel_in, lam_in, y_out):
    n_slabs = slabs.shape[0]
    rel_rows = nc.dram_tensor("rel_rows", (8, E_LEN), F32, kind="Internal").ap()
    with ExitStack() as stack:
        def sb(name, shape, dt=F32, scope=stack):
            return scope.enter_context(nc.sbuf_tensor(name, [P] + list(shape), dt))

        def sem(name):
            return stack.enter_context(nc.semaphore(name))

        G = stack.enter_context(nc.psum_tensor("gemm_banks", [P, 2, S], F32))
        SC = stack.enter_context(nc.psum_tensor("score_banks", [P, 2, S], F32))
        TR = stack.enter_context(nc.psum_tensor("turned_banks", [P, 2, S], F32))
        OB = stack.enter_context(nc.psum_tensor("out_banks", [P, 2, S], F32))

        x = sb("x", [KT, S])
        h_hi, h_lo = sb("h_hi", [KT, S], F32R), sb("h_lo", [KT, S], F32R)
        u_hi, u_lo = sb("u_hi", [KT, S], F32R), sb("u_lo", [KT, S], F32R)
        raw = sb("raw", [2, SLAB])
        w_hi, w_lo = sb("w_hi", [2, SLAB], F32R), sb("w_lo", [2, SLAB], F32R)
        cos1, sin1, cos2, sin2 = (sb(n, [S]) for n in ("cos1", "sin1", "cos2", "sin2"))
        consts, params = sb("consts", [N_CONST]), sb("params", [N_PARAM])
        ident_r, anti_r, causal_r, strict_r, chunk_r = (
            sb(n, [P], F32R) for n in ("ident_r", "anti_r", "causal_r", "strict_r", "chunk_r"))
        QT, KTT, V = sb("QT", [2, S]), sb("KT", [2, S]), sb("V", [2, NB, P])
        VT = sb("VT", [S])
        prob, turned = sb("prob", [2, S]), sb("turned", [2, S])
        On = sb("On", [2, NB, P])
        tmp = sb("tmp", [4, S])
        row_max, row_sum = sb("row_max", [4]), sb("row_sum", [2, 16])
        inv, inv2, small = sb("inv", [16]), sb("inv2", [16]), sb("small", [32])
        neg_lam = sb("neg_lam", [1])

        def scope():
            return stack.enter_context(ExitStack())
        region = ExitStack()
        fox_a = sb("fox_a", [S], F32R, region)
        fox_b = sb("fox_b", [8, S], F32R, region)
        t_raw = sb("t_raw", [2, S], F32, region)
        t_hi, t_lo = sb("t_hi", [2, S], F32R, region), sb("t_lo", [2, S], F32R, region)
        region.close()
        region = ExitStack()
        cn_hi, cn_lo = sb("cn_hi", [C_TILES, S], F32R, region), sb("cn_lo", [C_TILES, S], F32R, region)
        kr = sb("kr", [S], F32, region)
        inner = ExitStack()
        c_raw = sb("c_raw", [C_TILES, S], F32, inner)
        inner.close()
        QM, KM = sb("QM", [2, S], F32, region), sb("KM", [2, S], F32, region)
        region.close()
        region = ExitStack()
        K_sel, K_win = sb("K_sel", [S], F32, region), sb("K_win", [S], F32, region)
        V_sel, V_win = sb("V_sel", [NB, P], F32, region), sb("V_win", [NB, P], F32, region)
        K_cmp, V_cmp, V_cmpT = sb("K_cmp", [32], F32, region), sb("V_cmp", [P], F32, region), sb("V_cmpT", [32], F32, region)
        gates = sb("gates", [NB, 24], F32, region)
        x2 = sb("x2", [2, S], F32, region)
        blk = sb("blk", [CMP_M, CC], F32, region)
        blk_hi, blk_lo = sb("blk_hi", [CMP_M, CC], F32R, region), sb("blk_lo", [CMP_M, CC], F32R, region)
        hid, hid_e = sb("hid", [2, CC], F32, region), sb("hid_e", [2, CC], F32, region)
        region.close()
        region = ExitStack()
        m_hi, m_lo = sb("m_hi", [KT, S], F32R, region), sb("m_lo", [KT, S], F32R, region)
        region.close()
        hold = stack.enter_context(nc.sbuf_tensor("region_m", [P, 2 * KT * S + 4], F32))
        del hold
        region = ExitStack()
        sq, acc, rstd = sb("sq", [2, S], F32, region), sb("acc", [S], F32, region), sb("rstd", [S], F32, region)
        region.close()
        region = ExitStack()
        soft, spl, suffix = sb("soft", [2, S], F32, region), sb("spl", [S], F32, region), sb("suffix", [S], F32, region)
        region.close()
        region = ExitStack()
        sc_c = sb("sc_c", [8, CMP_BLOCKS], F32, region)
        pc = sb("pc", [8, CMP_BLOCKS], F32, region)
        pcT = sb("pcT", [2, S], F32, region)
        region.close()
        hold = stack.enter_context(nc.sbuf_tensor("region_n", [P, 4 * S], F32))
        del hold

        ident, ones = consts[:, CO["ident"]], consts[:, CO["ones"]]

        x_landed = [sem("x_landed0"), sem("x_landed1")]
        small_landed, pos_landed = sem("small_landed"), sem("pos_landed")
        rel_landed, rel_stored, t_landed = sem("rel_landed"), sem("rel_stored"), sem("t_landed")
        raw_landed = [sem("raw_landed0"), sem("raw_landed1")]
        slab_hi, slab_split = sem("slab_hi"), sem("slab_split")
        gemm_full, gemm_free = sem("gemm_full"), sem("gemm_free")
        act_hi, act_lo = sem("act_hi"), sem("act_lo")
        s_full, s_seen, p_ready = sem("s_full"), sem("s_seen"), sem("p_ready")
        pt_full, pt_ready, pv_done = sem("pt_full"), sem("pt_ready"), sem("pv_done")
        o_ready, sq_ready, acc_ready = sem("o_ready"), sem("sq_ready"), sem("acc_ready")
        rstd_ready = sem("rstd_ready")
        swapped, rope_ready, ln_ready = sem("swapped"), sem("rope_ready"), sem("ln_ready")
        dve_step, act_step = sem("dve_step"), sem("act_step")
        rel_ready, masks_ready, fox_ready = sem("rel_ready"), sem("masks_ready"), sem("fox_ready")
        t_hi_ready, t_ready, y_stored = sem("t_hi_ready"), sem("t_ready"), sem("y_stored")
        angles_ready, sines_ready = sem("angles_ready"), sem("sines_ready")
        gates_in, gates_soft, lam_in_ready, lam_exp = sem("gates_in"), sem("gates_soft"), sem("lam_sums"), sem("lam_exp")
        h32_ready, w1_used, kr_ready = sem("h32_ready"), sem("w1_used"), sem("kr_ready")
        x2_ready, blk_ready, blk_hi_ready = sem("x2_ready"), sem("blk_ready"), sem("blk_hi_ready")
        logits_ready, pc_exp, pc_ready = sem("logits_ready"), sem("pc_exp"), sem("pc_ready")
        norm2_in, norm2_out = sem("norm2_in"), sem("norm2_out")

        block = stack.enter_context(nc.Block())

        @block.sync
        def _(sp):
            for j in range(2):
                sp.dma_start(raw[:, j, :], slabs[j]).then_inc(raw_landed[j], 16)
            with sp.Fori(1, n_slabs // 2) as i:
                for j in range(2):
                    sp.wait_ge(slab_split, i * 2 + (j - 1))
                    sp.dma_start(raw[:, j, :], slabs[i * 2 + j]).then_inc(raw_landed[j], 16)

        @block.gpsimd
        def _(pool):
            with pool.Fori(0, n_slabs // 2) as i:
                for j in range(2):
                    pool.wait_ge(slab_hi, i * 2 + (j + 1))
                    pool.tensor_tensor(w_lo[:, j, :], raw[:, j, :], w_hi[:, j, :].bitcast(F32),
                                       ALU.subtract).then_inc(slab_split, 1)

        @block.tensor
        def _(pe):
            c = Counts()

            def open_bank():
                if c.gemm.past(1):
                    pe.wait_ge(gemm_free, c.gemm.at(-1))
                return G[:, c.gemm.slot, :]

            def product(out, kt, width, rhs_hi, rhs_lo, first, last, col=None):
                col = kt * P if col is None else col
                w = slice(col, col + width)
                high, low = w_hi[:, c.slab.slot, w], w_lo[:, c.slab.slot, w]
                pe.matmul(out, high, rhs_hi, start=first, stop=False)
                pe.matmul(out, high, rhs_lo, start=False, stop=False)
                return pe.matmul(out, low, rhs_hi, start=False, stop=last)

            def gemm_slab(hi, lo, tiles=KT, width=P, fresh=0, ready=None):
                bank = open_bank()
                pe.wait_ge(slab_split, c.slab.at(1))
                for kt in range(tiles):
                    if fresh:
                        pe.wait_ge(act_lo, c.lo.at(kt + 1))
                    last = product(bank[0:width, :], kt, width, hi[:, kt, :], lo[:, kt, :],
                                   kt == 0, kt == tiles - 1)
                last.then_inc(gemm_full, 1)
                c.slab.now += 1
                c.gemm.now += 1
                if fresh:
                    c.lo.now += tiles

            def norm_sum(tiles=0):
                bank = open_bank()
                c.acc.now += tiles
                pe.wait_ge(acc_ready, c.acc.at())
                pe.matmul(bank, ones, acc[:, :], start=True, stop=True).then_inc(gemm_full, 1)
                c.gemm.now += 1

            def turn(src, rows=P, blocks=NB, width=P, out_rows=P):
                bank = open_bank()
                for j in range(blocks):
                    last = pe.transpose(bank[0:width, j * rows:(j + 1) * rows],
                                        src(j), ident[0:rows, 0:rows])
                last.then_inc(gemm_full, 1)
                c.gemm.now += 1

            def turn_v(behind=0):
                pe.wait_ge(gemm_free, c.gemm.at(-behind))
                turn(lambda j: VT[:, j * P:(j + 1) * P])

            def turn_out(slot):
                pe.wait_ge(o_ready, c.out.at(1))
                turn(lambda j: On[:, slot, j, :])
                c.out.now += 1

            def project(proj, slot, slots, latent=False):
                for name, j, n, ends in work(proj, slot, slots):
                    if name == "vt":
                        turn_v(1 if proj is PLAIN else 0)
                        continue
                    if j == 0:
                        open_bank()
                        if not (latent and name[0] == "k"):
                            pe.wait_ge(slab_split, c.slab.at(1))
                    bank = G[:, c.gemm.slot, :]
                    if latent:
                        kt = j + (Q_TILES if name[0] == "k" else 0)
                        last = product(bank, kt, P, cn_hi[:, kt, :], cn_lo[:, kt, :], j == 0, j == n - 1)
                    else:
                        last = product(bank, j, P, h_hi[:, j, :], h_lo[:, j, :], j == 0, j == n - 1)
                    if j == n - 1:
                        last.then_inc(gemm_full, 1)
                        c.gemm.now += 1
                    if ends:
                        c.slab.now += 1

            def attend(steps, qk, mask, value, out, bias=None, proj=(), latent=False, lags=(1, 2),
                       free=1, opens=(0,), roped=False, behind=0):
                lag_b, lag_c = lags
                n, slots = len(steps), len(steps) + lag_c
                for s in range(slots):
                    if s < n:
                        head, i = steps[s]
                        w = (i + 1) * P
                        if s == 0:
                            if roped:
                                pe.wait_ge(rope_ready, c.rope.at())
                            pe.wait_ge(gemm_free, c.gemm.at(-behind))
                        q, k = qk(head)
                        slot = (c.step.now + s) % 2
                        if c.step.past(1 - s):
                            pe.wait_ge(p_ready, c.step.at(s - 1))
                        pe.matmul(SC[:, slot, 0:w], q[:, i * P:(i + 1) * P], k[:, 0:w],
                                  start=True, stop=False, skip_group_check=True)
                        if bias is not None:
                            bias(head, i, SC[:, slot, 0:w])
                        pe.matmul(SC[:, slot, i * P:w], ident_r[:, :], mask[:, :], start=False, stop=True,
                                  skip_group_check=True).then_inc(s_full, 1)
                    if proj:
                        project(proj, s, slots, latent)
                    t = s - lag_b
                    if 0 <= t < n:
                        head, i = steps[t]
                        slot = (c.step.now + t) % 2
                        pe.wait_ge(p_ready, c.step.at(t + 1))
                        if c.step.past(1 - t):
                            pe.wait_ge(pt_ready, c.step.at(t - 1))
                        for j in range(i + 1):
                            last = pe.transpose(TR[:, slot, j * P:(j + 1) * P],
                                                prob[:, slot, j * P:(j + 1) * P], ident)
                        last.then_inc(pt_full, 1)
                    t = s - lag_c
                    if 0 <= t < n:
                        head, i = steps[t]
                        slot = (c.step.now + t) % 2
                        pe.wait_ge(pt_ready, c.step.at(t + 1))
                        if t in opens and c.out.past(free):
                            pe.wait_ge(o_ready, c.out.at(-free))
                        for j in range(i + 1):
                            last = pe.matmul(out(head, i), turned[:, slot, j * P:(j + 1) * P],
                                             value(head, j), start=(j == 0), stop=(j == i),
                                             skip_group_check=True)
                        last.then_inc(pv_done, 1)
                c.step.now += n

            STEPS = [(h, i) for h in range(2) for i in range(NB)]

            def pair_qk(par, keys=None):
                def qk(head):
                    rows = slice(64 * head, 64 * head + 64)
                    k = KTT[rows, par, :] if keys is None else keys[rows, :]
                    return QT[rows, par, :], k
                return qk

            def pair_out(par):
                return lambda head, i: OB[:, par, i * P + head * HEAD:i * P + (head + 1) * HEAD]

            def pair_value(par):
                return lambda head, j: V[:, par, j, head * HEAD:(head + 1) * HEAD]

            def pairs(mask, proj, bias=lambda par: None, qk=pair_qk, latent=False, lags=(1, 2)):
                project(proj, 0, 1, latent)
                for par in range(2):
                    attend(STEPS, qk(par), mask, pair_value(par), pair_out(par), bias(par),
                           proj if par == 0 else (), latent, lags, behind=par)
                    turn_out(par)

            pe.wait_ge(small_landed, 32)
            norm_sum(KT)
            gemm_slab(h_hi, h_lo, width=8, fresh=1)
            pe.wait_ge(masks_ready, 5)

            with c.loop(pe, 2, slab=6, gemm=10, step=16, out=2) as it:
                def forget(par):
                    def add(head, i, out):
                        if par == 0 and head == 0 and i == 0:
                            pe.wait_ge(fox_ready, 8)
                        pe.matmul(out, fox_a[:, i * P:(i + 1) * P],
                                  fox_b[:, it * 4 + (2 * par + head), 0:(i + 1) * P],
                                  start=False, stop=False, skip_group_check=True)
                    return add
                pairs(causal_r, PLAIN, forget)

            with c.loop(pe, 2, slab=6, gemm=10, step=16, out=2) as it:
                def relative(par):
                    def add(head, i, out):
                        if head == 0 and i == 0:
                            pe.wait_ge(t_ready, it * 2 + (par + 1))
                        cols = slice(384 - i * P, S)
                        for t in (t_hi, t_lo):
                            pe.matmul(out, anti_r[:, :], t[:, head, cols], start=False, stop=False,
                                      skip_group_check=True)
                    return add
                pairs(chunk_r, PLAIN, relative)

            def project_out(hi, lo, tiles=KT):
                for n in range(KT):
                    gemm_slab(hi, lo, tiles)
                c.acc.now += KT

            def mlp():
                with c.loop(pe, 4, slab=16, gemm=16, lo=8, acc=8):
                    for j in range(8):
                        gemm_slab(h_hi, h_lo)
                    gemm_slab(u_hi, u_lo, fresh=1)
                    for j in range(7):
                        gemm_slab(u_hi, u_lo)
                    c.acc.now += KT

            pe.wait_ge(gemm_free, c.gemm.at())
            project_out(u_hi, u_lo)
            norm_sum()
            pe.wait_ge(act_lo, c.lo.at(KT))
            c.lo.now += KT
            mlp()

            norm_sum()
            gemm_slab(h_hi, h_lo, fresh=1)
            for j in range(Q_TILES - 1):
                gemm_slab(h_hi, h_lo)
            gemm_slab(h_hi, h_lo, width=64)
            norm_sum(Q_TILES)
            for j in range(KV_TILES):
                gemm_slab(h_hi, h_lo)
            norm_sum(KV_TILES)
            with c.loop(pe, 2, slab=6, gemm=10, step=16, out=2):
                pairs(strict_r, PLAIN, lags=(2, 3))

            def latent_qk(par):
                return lambda head: ((QT, QM)[head][0:96, par, :], (KTT, KM)[head][0:96, par, :])

            pe.wait_ge(act_lo, c.lo.at(C_TILES))
            c.lo.now += C_TILES
            pe.wait_ge(kr_ready, 1)
            with c.loop(pe, 2, slab=4, gemm=12, step=16, out=2):
                pairs(chunk_r, LATENT, qk=latent_qk, latent=True)
            pe.wait_ge(gemm_free, c.gemm.at())
            project_out(u_hi, u_lo)
            norm_sum()
            pe.wait_ge(act_lo, c.lo.at(KT))
            c.lo.now += KT
            mlp()

            norm_sum()
            norm_sum(KT)
            gemm_slab(h_hi, h_lo, fresh=1)
            gemm_slab(h_hi, h_lo)
            for kv, w2 in enumerate(("w2_k", "w2_v")):
                pe.wait_ge(act_lo, c.lo.at(1))
                c.lo.now += 1
                banks = []
                for t in range(2):
                    banks.append(open_bank())
                    c.gemm.now += 1
                for q in range(4):
                    pe.wait_ge(slab_split, c.slab.at(1))
                    for m in range(4 * q, 4 * q + 4):
                        for t in range(2):
                            last = product(banks[t][:, 0:CC], 0, P, blk_hi[:, m, :], blk_lo[:, m, :],
                                           m == 0, m == CMP_M - 1, col=(m % 4) * 256 + t * P)
                            if m == CMP_M - 1:
                                last.then_inc(gemm_full, 1)
                    if q < 3:
                        last.then_inc(w1_used, 1)
                    c.slab.now += 1
                bank = open_bank()
                pe.wait_ge(gemm_free, c.gemm.at())
                w2c = PC[w2].start
                for t in range(2):
                    last = pe.matmul(bank[0:64, 0:CC], params[:, w2c + 64 * t:w2c + 64 * t + 64],
                                     hid[:, t, :], start=(t == 0), stop=(t == 1))
                last.then_inc(gemm_full, 1)
                c.gemm.now += 1
            pe.wait_ge(gemm_free, c.gemm.at())
            bank = open_bank()
            pe.transpose(bank[0:CMP_BLOCKS, 0:P], V_cmpT[:, 0:CMP_BLOCKS], ident).then_inc(gemm_full, 1)
            c.gemm.now += 1
            for branch in range(2):
                gemm_slab(h_hi, h_lo)
                gemm_slab(h_hi, h_lo)
                turn_v()
            gemm_slab(h_hi, h_lo, width=24)
            pe.wait_ge(gemm_free, c.gemm.at())
            bank = open_bank()
            for j in range(NB):
                last = pe.transpose(bank[:, j * 24:(j + 1) * 24], VT[0:24, j * P:(j + 1) * P],
                                    ident[0:24, 0:24])
            last.then_inc(gemm_full, 1)
            c.gemm.now += 1

            c.rope.now += 3

            with c.loop(pe, 2, slab=6, gemm=10, step=16, out=2, rope=4):
                project(ROPED, 0, 1)
                c.rope.now += 2
                for par in range(2):
                    attend(STEPS, pair_qk(par), causal_r, lambda head, j, par=par: V[:, par, j, :],
                           lambda head, i: OB[:, head, i * P:(i + 1) * P], None,
                           ROPED if par == 0 else (), free=0, roped=True, behind=par)
                    if par == 0:
                        c.rope.now += 2
                    turn_out(par)

            with c.loop(pe, 2, slab=2, gemm=14, step=32, out=2, rope=2) as it:
                for par in range(2):
                    project(QUERY, 0, 1)
                    c.rope.now += 1
                    pe.wait_ge(rope_ready, c.rope.at())
                    for head in range(2):
                        bank = open_bank()
                        rows = slice(64 * head, 64 * head + 64)
                        for i in range(NB):
                            last = pe.matmul(bank[:, i * CMP_BLOCKS:(i + 1) * CMP_BLOCKS],
                                             QT[rows, par, i * P:(i + 1) * P], K_cmp[rows, 0:CMP_BLOCKS],
                                             start=True, stop=True)
                        last.then_inc(gemm_full, 1)
                        c.gemm.now += 1
                    both = [(br, head, i) for br in range(2) for head in range(2) for i in range(NB)]
                    keys, values = (K_sel, K_win), (V_sel, V_win)
                    attend([((br, head), i) for br, head, i in both],
                           lambda bh, par=par: pair_qk(par, keys[bh[0]])(bh[1]), causal_r,
                           lambda bh, j: values[bh[0]][:, j, bh[1] * HEAD:(bh[1] + 1) * HEAD],
                           lambda bh, i: OB[:, bh[0], i * P + bh[1] * HEAD:i * P + (bh[1] + 1) * HEAD],
                           free=0, behind=2)
                    for head in range(2):
                        bank = open_bank()
                        if head == 0:
                            pe.wait_ge(pc_ready, it * 2 + (par + 1))
                        for i in range(NB):
                            last = pe.transpose(bank[0:CMP_BLOCKS, i * P:(i + 1) * P],
                                                pc[:, head * NB + i, :], ident)
                        last.then_inc(gemm_full, 1)
                        c.gemm.now += 1
                    bank = open_bank()
                    pe.wait_ge(gemm_free, c.gemm.at())
                    for head in range(2):
                        for i in range(NB):
                            last = pe.matmul(bank[:, i * P + head * HEAD:i * P + (head + 1) * HEAD],
                                             pcT[0:CMP_BLOCKS, head, i * P:(i + 1) * P],
                                             V_cmp[0:CMP_BLOCKS, head * HEAD:(head + 1) * HEAD],
                                             start=True, stop=True)
                    last.then_inc(gemm_full, 1)
                    c.gemm.now += 1
                    turn_out(par)

            pe.wait_ge(gemm_free, c.gemm.at())
            with c.loop(pe, 4, slab=6, gemm=8):
                for j in range(2):
                    gemm_slab(h_hi, h_lo)
                    gemm_slab(h_hi, h_lo)
                    pe.wait_ge(slab_split, c.slab.at(1))
                    for branch in range(2):
                        bank = open_bank()
                        for kt in range(4):
                            t = 4 * branch + kt
                            last = product(bank, t, P, u_hi[:, t, :], u_lo[:, t, :], kt == 0, kt == 3)
                        last.then_inc(gemm_full, 1)
                        c.gemm.now += 1
                    c.slab.now += 1
            pe.wait_ge(act_lo, c.lo.at(8))
            c.lo.now += 8
            project_out(m_hi, m_lo)
            norm_sum()
            pe.wait_ge(act_lo, c.lo.at(KT))
            c.lo.now += KT

            def swiglu(tiles):
                c.acc.now += KT
                for j in range(2 * tiles):
                    gemm_slab(h_hi, h_lo)
                gemm_slab(u_hi, u_lo, tiles, fresh=1)
                for j in range(KT - 1):
                    gemm_slab(u_hi, u_lo, tiles)

            with c.loop(pe, 2, slab=24, gemm=24, lo=8, acc=8):
                swiglu(8)
            swiglu(FF2_TILES - 16)
            norm_sum()

        @block.scalar
        def _(act):
            c = Counts()

            def split(off=2):
                m = c.slab.now + off
                landed = 16 * (m // 2 + 1)
                for i, per in c.slab.loops:
                    landed = i * (8 * per) + landed
                act.wait_ge(raw_landed[m % 2], landed)
                act.activation(w_hi[:, m % 2, :], raw[:, m % 2, :], ACT.Copy).then_inc(slab_hi, 1)

            def slab_done():
                act.wait_ge(gemm_full, c.gemm.at())
                split()
                c.slab.now += 1

            def link(ins):
                ins.then_inc(act_step, 1)
                c.link.now += 1
                act.wait_ge(act_step, c.link.at())

            def square(src):
                if c.acc.past(1):
                    act.wait_ge(acc_ready, c.acc.at(-1))
                act.activation(sq[:, c.acc.slot, :], src, ACT.Square).then_inc(sq_ready, 1)
                c.acc.now += 1

            def rsqrt():
                act.wait_ge(gemm_free, c.gemm.at())
                link(act.activation(rstd[:, :], rstd[:, :], ACT.Ln))
                act.activation(rstd[:, :], rstd[:, :], ACT.Exp, scale=-0.5).then_inc(rstd_ready, 1)
                c.rstd.now += 1

            def round_norm(hi, tiles):
                for j in range(tiles):
                    act.wait_ge(h32_ready, c.h32.at(1))
                    act.activation(hi[:, j, :], tmp[:, j % 2, :], ACT.Copy).then_inc(act_hi, 1)
                    c.h32.now += 1
                    c.hi.now += 1

            def norm(hi):
                c.gemm.now += 1
                rsqrt()
                round_norm(hi, KT)

            def gemm_slab():
                c.gemm.now += 1
                slab_done()

            def out_slab(src):
                gemm_slab()
                act.wait_ge(gemm_free, c.gemm.at())
                square(src)

            def swap():
                act.wait_ge(gemm_free, c.gemm.at())
                for r in range(0, P, 32):
                    o = r ^ 32
                    last = act.activation(tmp[r:r + 32, 1, :], tmp[o:o + 32, 0, :], ACT.Copy)
                last.then_inc(swapped, 1)
                c.rope.now += 1

            def project(proj, slot, slots, roped=False):
                for name, j, n, ends in work(proj, slot, slots):
                    if name == "vt":
                        c.gemm.now += 1
                    elif j == n - 1:
                        c.gemm.now += 1
                        if ends:
                            slab_done()
                        if roped and name in "qk":
                            swap()

            def attend(steps, sums, proj=(), lag_c=2, roped=False, stick=False):
                n, slots = len(steps), len(steps) + lag_c
                for s in range(slots):
                    if s < n:
                        slot = (c.step.now + s) % 2
                        w = (steps[s][1] + 1) * P
                        if stick:
                            act.wait_ge(s_full, c.step.at(s + 1))
                            link(act.activation(soft[:, slot, 0:w], SC[:, slot, 0:w], ACT.Abs))
                            link(act.activation(soft[:, slot, 0:w], soft[:, slot, 0:w], ACT.Exp, scale=-1.0))
                            act.activation(soft[:, slot, 0:w], soft[:, slot, 0:w], ACT.Ln,
                                           bias=ones[:, 0:1]).then_inc(ln_ready, 1)
                        else:
                            act.wait_ge(s_seen, c.step.at(s + 1))
                            if c.step.past(1 - s):
                                act.wait_ge(pt_full, c.step.at(s - 1))
                            act.activation(prob[:, slot, 0:w], SC[:, slot, 0:w], ACT.Exp,
                                           bias=row_max[:, (c.step.now + s) % 4:(c.step.now + s) % 4 + 1],
                                           accum_out=row_sum[:, sums, s:s + 1]).then_inc(p_ready, 1)
                    t = s - 1
                    if stick and 0 <= t < n:
                        slot = (c.step.now + t) % 2
                        w = (steps[t][1] + 1) * P
                        act.wait_ge(s_seen, c.step.at(t + 1))
                        if c.step.past(1 - t):
                            act.wait_ge(pt_full, c.step.at(t - 1))
                        act.activation(prob[:, slot, 0:w], soft[:, slot, 0:w], ACT.Exp).then_inc(p_ready, 1)
                    if proj:
                        project(proj, s, slots, roped)
                c.step.now += n

            STEPS = [(h, i) for h in range(2) for i in range(NB)]

            def pairs(proj, after=lambda par: None, stick=False):
                project(proj, 0, 1)
                for par in range(2):
                    attend(STEPS, par, proj if par == 0 else (), 3 if stick else 2, stick=stick)
                    after(par)
                    c.gemm.now += 1
                    c.out.now += 1

            act.dma_start(consts[:, :], consts_in).then_inc(small_landed, 16)
            act.dma_start(x[:, 0:4, :], x_in[0:512, :].rearrange("(t p) s -> p t s", p=P)).then_inc(x_landed[0], 16)
            act.dma_start(x[:, 4:8, :], x_in[512:1024, :].rearrange("(t p) s -> p t s", p=P)).then_inc(x_landed[1], 16)
            act.dma_start(params[:, :], params_in).then_inc(small_landed, 16)
            pos = On[:, :, :, :].rearrange("p a b c -> p (a b c)").bitcast(I32)
            act.dma_start(pos[:, 0:S], pos1_in.partition_broadcast(P)).then_inc(pos_landed, 16)
            act.dma_start(pos[:, S:2 * S], pos2_in.partition_broadcast(P)).then_inc(pos_landed, 16)
            act.dma_start(VT[:, 0:256], lam_in.partition_broadcast(P)).then_inc(pos_landed, 16)
            act.dma_start(prob[0:8, 0, 0:N_REL], rel_in).then_inc(rel_landed, 16)

            act.preload_act_table_set("natural_log_exp_and_others")
            split(0)
            split(1)
            for j in range(KT):
                act.wait_ge(x_landed[j // 4], 16)
                square(x[:, j, :])
            norm(h_hi)

            for n, (cosine, sine) in enumerate(((cos1, sin1), (cos2, sin2))):
                act.wait_ge(angles_ready, n + 1)
                act.activation(sine[:, :], tmp[:, 1, :], ACT.Sin)
                link(act.activation(tmp[:, 3, :], tmp[:, 1, :], ACT.Abs))
                act.activation(cosine[:, :], tmp[:, 3, :], ACT.Sin, scale=-1.0,
                               bias=consts[:, CO["half_pi"]]).then_inc(sines_ready, 1)
            act.preload_act_table_set("natural_log_exp_and_others")
            act.wait_ge(lam_in_ready, 1)
            act.activation(small[:, 2:4], small[:, 0:2], ACT.Exp).then_inc(lam_exp, 1)

            gemm_slab()
            act.wait_ge(gemm_free, c.gemm.at())
            link(act.activation(tmp[0:8, 1, :], tmp[0:8, 0, :], ACT.Abs))
            link(act.activation(tmp[0:8, 1, :], tmp[0:8, 1, :], ACT.Exp, scale=-1.0))
            act.activation(tmp[0:8, 1, :], tmp[0:8, 1, :], ACT.Ln, bias=ones[0:8, 0:1]).then_inc(gates_soft, 1)

            act.wait_ge(rel_ready, 3)
            act.dma_start(rel_rows, t_raw[0:8, :, :].rearrange("p a b -> p (a b)")[:, 0:E_LEN]).then_inc(rel_stored, 16)
            act.wait_ge(rel_stored, 16)

            with c.loop(act, 2, slab=6, gemm=10, step=16, out=2):
                pairs(PLAIN)

            def load_bias(pair):
                act.dma_start(t_raw[:, :, :], bass.AP(rel_rows.tensor, pair * (2 * E_LEN),
                                                     [[1, P], [E_LEN, 2], [1, S]])).then_inc(t_landed, 16)

            with c.loop(act, 2, slab=6, gemm=10, step=16, out=2) as it:
                def round_bias(k):
                    act.wait_ge(t_landed, it * 32 + 16 * (k + 1))
                    act.activation(t_hi[:, :, :], t_raw[:, :, :], ACT.Copy).then_inc(t_hi_ready, 1)
                load_bias(it * 2)
                round_bias(0)

                def next_bias(par):
                    if par == 0:
                        act.wait_ge(t_ready, it * 2 + 1)
                        load_bias(it * 2 + 1)
                        round_bias(1)
                pairs(PLAIN, next_bias)

            def project_out():
                for j in range(KT):
                    out_slab(x[:, j, :])

            def square_relu():
                gemm_slab()
                act.wait_ge(gemm_free, c.gemm.at())
                s = (c.gemm.now - 1) % 2
                link(act.activation(tmp[:, 2 + s, :], tmp[:, s, :], ACT.Square))

            def mlp():
                with c.loop(act, 4, slab=16, gemm=16, hi=8, acc=8, link=8):
                    for j in range(8):
                        square_relu()
                        act.activation(u_hi[:, j, :], tmp[:, 2 + (c.gemm.now - 1) % 2, :],
                                       ACT.Copy).then_inc(act_hi, 1)
                        c.hi.now += 1
                    for j in range(KT):
                        out_slab(x[:, j, :])

            project_out()
            norm(h_hi)
            mlp()

            norm(h_hi)
            for j in range(Q_TILES):
                out_slab(c_raw[:, j, :])
            gemm_slab()
            c.gemm.now += 1
            rsqrt()
            out_slab(c_raw[:, Q_TILES, :])
            round_norm(cn_hi, Q_TILES)
            out_slab(c_raw[:, Q_TILES + 1, :])
            c.gemm.now += 1
            rsqrt()
            round_norm(cn_hi[:, Q_TILES:, :], KV_TILES)
            with c.loop(act, 2, slab=6, gemm=10, step=16, out=2, link=32):
                pairs(PLAIN, stick=True)
            with c.loop(act, 2, slab=4, gemm=12, step=16, out=2):
                pairs(LATENT)
            project_out()
            norm(h_hi)
            mlp()

            c.gemm.now += 1
            rsqrt()
            for j in range(KT):
                act.wait_ge(h32_ready, c.h32.at(1))
                c.h32.now += 1
                square(x[:, j, :])
            norm(h_hi)
            gemm_slab()
            swap()
            gemm_slab()
            for kv in range(2):
                src = KTT[:, kv, :]
                if kv == 0:
                    act.wait_ge(rope_ready, c.rope.at())
                else:
                    act.wait_ge(gemm_free, c.gemm.at(-3))
                    act.wait_ge(blk_ready, 1)
                for g in range(2):
                    rows = slice(64 * g, 64 * g + 64)
                    act.activation(x2[0:64, g, :], src[rows, :], ACT.Copy).then_inc(x2_ready, 1)
                    act.activation(x2[64:128, g, 0:S - 1], src[rows, 1:S], ACT.Copy).then_inc(x2_ready, 1)
                act.wait_ge(blk_ready, kv + 1)
                act.activation(blk_hi[:, :, :], blk[:, :, :], ACT.Copy).then_inc(blk_hi_ready, 1)
                for q in range(3):
                    act.wait_ge(w1_used, 3 * kv + q + 1)
                    split()
                    c.slab.now += 1
                c.gemm.now += 2
                slab_done()
                for t in range(2):
                    act.activation(hid[:, t, :], G[:, (c.gemm.now + t) % 2, 0:CC], ACT.Silu).then_inc(gemm_free, 1)
                c.gemm.now += 1
            c.gemm.now += 1
            for branch in range(2):
                gemm_slab()
                swap()
                gemm_slab()
                c.gemm.now += 1
            gemm_slab()
            act.wait_ge(gemm_free, c.gemm.at(-1))
            act.activation(VT[0:24, :], G[0:24, (c.gemm.now - 1) % 2, :], ACT.Sigmoid).then_inc(gemm_free, 1)
            c.gemm.now += 1
            act.preload_act_table_set("natural_log_exp_and_others")

            with c.loop(act, 2, slab=6, gemm=10, step=16, out=2, rope=4, link=2) as it:
                project(ROPED, 0, 1, True)
                for par in range(2):
                    attend(STEPS, par, ROPED if par == 0 else (), roped=True)
                    act.wait_ge(norm2_in, it * 2 + (par + 1))
                    link(act.activation(small[:, 4:8], small[:, 4:8], ACT.Ln))
                    act.activation(small[:, 4:8], small[:, 4:8], ACT.Exp, scale=-0.5).then_inc(norm2_out, 1)
                    c.gemm.now += 1
                    c.out.now += 1

            with c.loop(act, 2, slab=2, gemm=14, step=32, out=2, rope=2) as it:
                for par in range(2):
                    project(QUERY, 0, 1, True)
                    c.gemm.now += 2
                    act.wait_ge(logits_ready, it * 2 + (par + 1))
                    act.activation(pc[:, :, :], sc_c[:, :, :], ACT.Exp).then_inc(pc_exp, 1)
                    attend([(h, i) for h in range(4) for i in range(NB)], par)
                    c.gemm.now += 4
                    c.out.now += 1

            act.preload_act_table(ACT.Sigmoid)
            with c.loop(act, 4, slab=6, gemm=8):
                for j in range(2):
                    for k in range(2):
                        gemm_slab()
                        act.wait_ge(gemm_free, c.gemm.at(-1))
                        act.activation(tmp[:, k, :], G[:, (c.gemm.now - 1) % 2, :],
                                       ACT.Sigmoid).then_inc(gemm_free, 1)
                    c.gemm.now += 2
                    slab_done()
            act.preload_act_table_set("natural_log_exp_and_others")
            project_out()
            norm(h_hi)
            act.preload_act_table(ACT.Silu)

            def swiglu(tiles):
                for j in range(tiles):
                    gemm_slab()
                    act.activation(tmp[:, j % 2, :], G[:, (c.gemm.now - 1) % 2, :],
                                   ACT.Silu).then_inc(gemm_free, 1)
                    gemm_slab()
                    act.wait_ge(gemm_free, c.gemm.at())
                    act.activation(u_hi[:, j, :], tmp[:, 2 + j % 2, :], ACT.Copy).then_inc(act_hi, 1)
                    c.hi.now += 1
                for j in range(KT):
                    if tiles < 8 and c.slab.now + 2 >= n_slabs:
                        c.gemm.now += 1
                        c.slab.now += 1
                        act.wait_ge(gemm_free, c.gemm.at())
                        square(x[:, j, :])
                    else:
                        out_slab(x[:, j, :])

            with c.loop(act, 2, slab=24, gemm=24, hi=8, acc=8):
                swiglu(8)
            swiglu(FF2_TILES - 16)
            act.preload_act_table_set("natural_log_exp_and_others")
            c.gemm.now += 1
            rsqrt()
            for j in range(KT):
                act.wait_ge(h32_ready, c.h32.at(1))
                c.h32.now += 1
                act.dma_start(y_out[j * P:(j + 1) * P, :], x[:, j, :]).then_inc(y_stored, 16)
            act.wait_ge(y_stored, 16 * KT)

        @block.vector
        def _(dve):
            c = Counts()

            def link(ins):
                ins.then_inc(dve_step, 1)
                c.link.now += 1
                dve.wait_ge(dve_step, c.link.at())

            def result(rows=slice(0, P), cols=slice(0, S)):
                dve.wait_ge(gemm_full, c.gemm.at(1))
                bank = G[rows, c.gemm.slot, cols]
                c.gemm.now += 1
                return bank

            def move(dst, rows=slice(0, P), cols=slice(0, S)):
                dve.tensor_copy(dst, result(rows, cols)).then_inc(gemm_free, 1)
                dve.wait_ge(gemm_free, c.gemm.at())

            def scaled(dst, by):
                dve.tensor_scalar(dst, result(), by, None, ALU.mult).then_inc(gemm_free, 1)
                dve.wait_ge(gemm_free, c.gemm.at())

            def add_square(first):
                dve.wait_ge(sq_ready, c.acc.at(1))
                if first:
                    dve.tensor_copy(acc[:, :], sq[:, c.acc.slot, :]).then_inc(acc_ready, 1)
                else:
                    dve.wait_ge(acc_ready, c.acc.at())
                    dve.tensor_tensor(acc[:, :], acc[:, :], sq[:, c.acc.slot, :], ALU.add).then_inc(acc_ready, 1)
                c.acc.now += 1

            def normed(src, gain, dst):
                dve.scalar_tensor_tensor(dst, src, gain, rstd[:, :], ALU.mult, ALU.mult).then_inc(h32_ready, 1)
                c.h32.now += 1
                dve.wait_ge(h32_ready, c.h32.at())

            def norm_tiles(src, gains, hi, lo, tiles):
                dve.wait_ge(rstd_ready, c.rstd.at(1))
                c.rstd.now += 1
                g = PC[gains].start
                normed(src[:, 0, :], params[:, g:g + 1], tmp[:, 0, :])
                for j in range(tiles):
                    if j + 1 < tiles:
                        normed(src[:, j + 1, :], params[:, g + j + 1:g + j + 2], tmp[:, (j + 1) % 2, :])
                    dve.wait_ge(act_hi, c.hi.at(1))
                    dve.tensor_tensor(lo[:, j, :], tmp[:, j % 2, :], hi[:, j, :].bitcast(F32),
                                      ALU.subtract).then_inc(act_lo, 1)
                    c.lo.now += 1
                    dve.wait_ge(act_lo, c.lo.at())
                    c.hi.now += 1

            def norm(gains):
                mean(D)
                norm_tiles(x, gains, h_hi, h_lo, KT)

            def mean(width):
                dve.tensor_scalar(rstd[:, :], result(), 1.0 / width, EPS, ALU.mult, ALU.add).then_inc(gemm_free, 1)
                dve.wait_ge(gemm_free, c.gemm.at())

            def add_out():
                for j in range(KT):
                    bank = result()
                    dve.tensor_tensor(x[:, j, :], bank, x[:, j, :], ALU.add).then_inc(gemm_free, 1)
                    dve.wait_ge(gemm_free, c.gemm.at())
                    add_square(j == 0)

            def rotate(dst, scale):
                move(tmp[:, 0, :])
                dve.wait_ge(swapped, c.rope.at(1))
                dve.scalar_tensor_tensor(tmp[:, 2, :], tmp[:, 0, :], scale, cos2[:, :], ALU.mult, ALU.mult)
                link(dve.scalar_tensor_tensor(tmp[:, 3, :], tmp[:, 1, :], scale, sin2[:, :], ALU.mult, ALU.mult))
                dve.tensor_tensor(dst, tmp[:, 2, :], tmp[:, 3, :], ALU.add).then_inc(rope_ready, 1)
                dve.wait_ge(rope_ready, c.rope.at(1))
                c.rope.now += 1

            def latent_query(dst):
                dve.wait_ge(gemm_full, c.gemm.at(1))
                bank = G[:, c.gemm.slot, :]
                c.gemm.now += 1
                dve.scalar_tensor_tensor(tmp[64:96, 0, :], bank[64:96, :], MLA_SCALE, cos1[64:96, :], ALU.mult, ALU.mult)
                dve.scalar_tensor_tensor(tmp[64:96, 1, :], bank[96:128, :], MLA_SCALE, sin1[96:128, :], ALU.mult, ALU.mult)
                link(dve.tensor_scalar(dst[0:64, :], bank[0:64, :], MLA_SCALE, None, ALU.mult))
                dve.tensor_tensor(dst[64:96, :], tmp[64:96, 0, :], tmp[64:96, 1, :], ALU.add).then_inc(gemm_free, 1)
                dve.wait_ge(gemm_free, c.gemm.at())

            def evacuate(name, par, roped):
                if name == "v":
                    move(VT[:, :])
                elif name == "vt":
                    move(V[:, par, :, :])
                elif roped:
                    rotate((QT if name == "q" else KTT)[:, par, :], QK_SCALE if name == "q" else 1.0)
                elif name == "q":
                    scaled(QT[:, par, :], QK_SCALE)
                elif name == "k":
                    move(KTT[:, par, :])
                elif name[0] == "q":
                    latent_query((QT, QM)[int(name[1])][:, par, :])
                else:
                    head = int(name[2])
                    dve.wait_ge(gemm_full, c.gemm.at(1))
                    bank = G[:, c.gemm.slot, :]
                    c.gemm.now += 1
                    dve.tensor_copy((KTT, KM)[head][0:64, par, :], bank[0:64, :])
                    dve.tensor_copy(VT[64 * head:64 * head + 64, :], bank[64:128, :]).then_inc(gemm_free, 1)
                    dve.wait_ge(gemm_free, c.gemm.at())

            def project(proj, slot, slots, par, roped=False):
                for name, j, n, ends in work(proj, slot, slots):
                    if name == "vt" or j == n - 1:
                        evacuate(name, par, roped)
                        if ends:
                            c.slab.now += 1

            def attend(steps, proj=(), par=0, lags=(1, 2), roped=False, stick=False):
                lag_b, lag_c = lags
                n, slots = len(steps), len(steps) + lag_c
                for s in range(slots):
                    if s < n:
                        slot = (c.step.now + s) % 2
                        w = (steps[s][1] + 1) * P
                        if stick:
                            dve.wait_ge(ln_ready, c.ln.at(1))
                            c.ln.now += 1
                            link(dve.scalar_tensor_tensor(spl[:, 0:w], SC[:, slot, 0:w], 0.0,
                                                          soft[:, slot, 0:w], ALU.max, ALU.add))
                            back = spl[:, 0:w][:, ::-1]
                            link(dve.tensor_tensor_scan(suffix[:, 0:w][:, ::-1], back, back, 0.0, ALU.add, ALU.max))
                            dve.tensor_tensor(soft[:, slot, 0:w], SC[:, slot, 0:w], suffix[:, 0:w],
                                              ALU.subtract).then_inc(s_seen, 1)
                        else:
                            dve.wait_ge(s_full, c.step.at(s + 1))
                            k = (c.step.now + s) % 4
                            dve.tensor_reduce(row_max[:, k:k + 1], SC[:, slot, 0:w], X, ALU.max,
                                              negate=True).then_inc(s_seen, 1)
                    if proj:
                        project(proj, s, slots, par, roped)
                    t = s - lag_b
                    if 0 <= t < n:
                        slot = (c.step.now + t) % 2
                        w = (steps[t][1] + 1) * P
                        dve.wait_ge(pt_full, c.step.at(t + 1))
                        dve.tensor_copy(turned[:, slot, 0:w], TR[:, slot, 0:w]).then_inc(pt_ready, 1)
                c.step.now += n
                dve.wait_ge(pv_done, c.step.at())

            STEPS = [(h, i) for h in range(2) for i in range(NB)]

            def by_head(ap):
                return ap.rearrange("p (i h d) -> p h i d", i=NB, h=2)

            def over(col, width):
                return col.rearrange("p (h i) -> p h i", h=2).unsqueeze(3).to_broadcast([P, 2, NB, width])

            def flat(par):
                return On[:, par, :, :].rearrange("p i c -> p (i c)")

            def turned_out(tile):
                bank = result()
                link(dve.tensor_scalar(u_hi[:, tile, :], bank, 1.0, None, ALU.mult))
                dve.tensor_tensor(u_lo[:, tile, :], bank, u_hi[:, tile, :].bitcast(F32),
                                  ALU.subtract).then_inc(gemm_free, 1)
                dve.wait_ge(gemm_free, c.gemm.at())
                c.out.now += 1

            def pairs(proj, it, base, before=lambda par: None, lags=(1, 2), stick=False):
                project(proj, 0, 1, 0)
                for par in range(2):
                    before(par)
                    attend(STEPS, proj if par == 0 else (), 1, lags, stick=stick)
                    if stick:
                        dve.tensor_copy(flat(par), OB[:, par, :]).then_inc(o_ready, 1)
                        dve.wait_ge(o_ready, c.out.at(1))
                    else:
                        link(dve.reciprocal(inv[:, 0:8], row_sum[:, par, 0:8]))
                        dve.tensor_tensor(by_head(flat(par)), by_head(OB[:, par, :]), over(inv[:, 0:8], HEAD),
                                          ALU.mult).then_inc(o_ready, 1)
                        dve.wait_ge(o_ready, c.out.at(1))
                    turned_out(it * 2 + (base + par))

            dve.wait_ge(small_landed, 32)
            for name, tile in (("ident", ident_r), ("anti", anti_r), ("causal", causal_r),
                               ("strict", strict_r), ("chunk", chunk_r)):
                dve.tensor_scalar(tile[:, :], consts[:, CO[name]], 1.0, None, ALU.mult).then_inc(masks_ready, 1)

            for j in range(KT):
                add_square(j == 0)
            norm("mix0")

            dve.wait_ge(pos_landed, 48)
            pos = On[:, :, :, :].rearrange("p a b c -> p (a b c)").bitcast(I32)
            for n, (cosine, sine, k) in enumerate(((cos1, sin1, "1"), (cos2, sin2, "2"))):
                if n:
                    dve.wait_ge(sines_ready, n)
                link(dve.tensor_copy(tmp[:, 0, :], pos[:, n * S:(n + 1) * S]))
                link(dve.tensor_scalar(tmp[:, 1, :], tmp[:, 0, :], consts[:, CO["freq" + k]], None, ALU.mult))
                link(dve.tensor_scalar(tmp[:, 2, :], tmp[:, 1, :], 1 / TWO_PI, ROUND, ALU.mult, ALU.add))
                link(dve.tensor_scalar(tmp[:, 2, :], tmp[:, 2, :], -ROUND, None, ALU.add))
                for part in PI_PARTS:
                    link(dve.scalar_tensor_tensor(tmp[:, 1, :], tmp[:, 2, :], -float(part), tmp[:, 1, :],
                                                  ALU.mult, ALU.add))
                dve.tensor_scalar(tmp[:, 1, :], tmp[:, 1, :], 3.1415925, -3.1415925, ALU.min,
                                  ALU.max).then_inc(angles_ready, 1)
            for n, (sine, k) in enumerate(((sin1, "1"), (sin2, "2"))):
                dve.wait_ge(sines_ready, n + 1)
                link(dve.tensor_scalar(sine[:, :], sine[:, :], consts[:, CO["sign" + k]], None, ALU.mult))

            lam = VT[:, 0:256].rearrange("p (a b d) -> p a b d", a=2, b=2)
            prods = VT[:, 256:384].rearrange("p (a d) -> p a d", a=2)
            link(dve.tensor_tensor(prods, lam[:, :, 0, :], lam[:, :, 1, :], ALU.mult))
            dve.tensor_reduce(small[:, 0:2], prods, X, ALU.add).then_inc(lam_in_ready, 1)
            dve.wait_ge(lam_exp, 1)
            link(dve.scalar_tensor_tensor(neg_lam[:, :], small[:, 3:4], -LAM_INIT, small[:, 2:3], ALU.add,
                                          ALU.subtract))

            dve.wait_ge(gemm_full, c.gemm.at(1))
            dve.tensor_scalar(tmp[0:8, 0, :], G[0:8, c.gemm.slot, :], params[0:8, PC["b_forget"]], None,
                              ALU.add).then_inc(gemm_free, 1)
            dve.wait_ge(gemm_free, c.gemm.at(1))
            c.gemm.now += 1
            c.slab.now += 1
            factors = turned[:, 0, :]
            dve.memset(fox_a[:, :].bitcast(F32), 0.0)
            dve.memset(factors[0:64, :], 1.0)
            link(dve.memset(factors[64:128, :], 0.0))
            dve.memset(fox_a[64:72, :].bitcast(F32), 1.0)
            link(dve.memset(fox_a[96:104, :].bitcast(F32), 1.0))
            dve.wait_ge(gates_soft, 1)
            link(dve.scalar_tensor_tensor(tmp[0:8, 2, :], tmp[0:8, 0, :], 0.0, tmp[0:8, 1, :], ALU.min,
                                          ALU.subtract))
            link(dve.tensor_tensor_scan(tmp[0:8, 3, :], tmp[0:8, 2, :], tmp[0:8, 2, :], 0.0, ALU.add, ALU.min))
            link(dve.tensor_scalar(fox_a[0:8, :], tmp[0:8, 3, :], 1.0, None, ALU.mult))
            link(dve.tensor_tensor(fox_a[32:40, :], tmp[0:8, 3, :], fox_a[0:8, :].bitcast(F32), ALU.subtract))
            dve.tensor_scalar(factors[64:72, :], fox_a[0:8, :].bitcast(F32), -1.0, None, ALU.mult)
            link(dve.tensor_scalar(factors[96:104, :], fox_a[32:40, :].bitcast(F32), -1.0, None, ALU.mult))
            oh = CO["onehot"].start
            for h in range(8):
                dve.tensor_scalar(fox_b[:, h, :], factors, consts[:, oh + h:oh + h + 1], None,
                                  ALU.mult).then_inc(fox_ready, 1)

            dve.wait_ge(rel_landed, 16)
            rel = prob[0:8, 0, 0:N_REL]
            rows = t_raw[0:8, :, :].rearrange("p a b -> p (a b)")
            dve.tensor_copy(rows[:, 0:255], rel[:, N_REL - 1:N_REL].to_broadcast([8, 255])).then_inc(rel_ready, 1)
            dve.tensor_copy(rows[:, 255:575], rel[:, ::-1]).then_inc(rel_ready, 1)
            dve.tensor_copy(rows[:, 575:E_LEN], rel[:, 0:1].to_broadcast([8, E_LEN - 575])).then_inc(rel_ready, 1)

            with c.loop(dve, 2, slab=6, gemm=10, step=16, out=2, link=LINKS["fox"]) as it:
                pairs(PLAIN, it, 0)
            with c.loop(dve, 2, slab=6, gemm=10, step=16, out=2, link=LINKS["chunked"]) as it:
                def split_bias(par):
                    dve.wait_ge(t_hi_ready, it * 2 + (par + 1))
                    if par:
                        pass
                    dve.tensor_tensor(t_lo[:, :, :], t_raw[:, :, :], t_hi[:, :, :].bitcast(F32),
                                      ALU.subtract).then_inc(t_ready, 1)
                pairs(PLAIN, it, 4, split_bias)

            def relu():
                s = c.gemm.slot
                dve.tensor_scalar(tmp[:, s, :], result(), 0.0, None, ALU.max).then_inc(gemm_free, 1)
                dve.wait_ge(gemm_free, c.gemm.at())
                c.slab.now += 1
                return s

            def split_u(j, s):
                dve.wait_ge(act_hi, c.hi.at(1))
                dve.tensor_tensor(u_lo[:, j, :], tmp[:, 2 + s, :], u_hi[:, j, :].bitcast(F32),
                                  ALU.subtract).then_inc(act_lo, 1)
                c.lo.now += 1
                dve.wait_ge(act_lo, c.lo.at())
                c.hi.now += 1

            def mlp():
                with c.loop(dve, 4, slab=16, gemm=16, hi=8, lo=8, acc=8):
                    for j in range(8):
                        split_u(j, relu())
                    add_out()
                    c.slab.now += 8

            add_out()
            norm("mlp0")
            mlp()

            norm("mix1")

            def latent(j, first):
                dve.tensor_copy(c_raw[:, j, :], result()).then_inc(gemm_free, 1)
                dve.wait_ge(gemm_free, c.gemm.at())
                add_square(first)

            for j in range(Q_TILES):
                latent(j, j == 0)
            dve.wait_ge(gemm_full, c.gemm.at(1))
            bank = G[:, c.gemm.slot, :]
            c.gemm.now += 1
            dve.tensor_tensor(tmp[0:32, 2, :], bank[0:32, :], cos1[0:32, :], ALU.mult)
            link(dve.tensor_tensor(tmp[0:32, 3, :], bank[32:64, :], sin1[32:64, :], ALU.mult))
            dve.tensor_tensor(kr[0:32, :], tmp[0:32, 2, :], tmp[0:32, 3, :], ALU.add).then_inc(gemm_free, 1)
            dve.wait_ge(gemm_free, c.gemm.at())
            mean(P * Q_TILES)
            dve.tensor_copy(c_raw[:, Q_TILES, :], result()).then_inc(gemm_free, 1)
            dve.wait_ge(gemm_free, c.gemm.at())
            add_square(True)
            norm_tiles(c_raw, "q_norm", cn_hi, cn_lo, Q_TILES)
            latent(Q_TILES + 1, False)
            mean(P * KV_TILES)
            norm_tiles(c_raw[:, Q_TILES:, :], "kv_norm", cn_hi[:, Q_TILES:, :], cn_lo[:, Q_TILES:, :], KV_TILES)
            with c.loop(dve, 2, slab=6, gemm=10, step=16, out=2, ln=16, link=LINKS["stick"]) as it:
                pairs(PLAIN, it, 0, lags=(2, 3), stick=True)
            for j, k in enumerate((KTT[64:96, 0, :], KTT[64:96, 1, :], KM[64:96, 0, :], KM[64:96, 1, :])):
                last = dve.tensor_copy(k, kr[0:32, :])
            last.then_inc(kr_ready, 1)
            with c.loop(dve, 2, slab=4, gemm=12, step=16, out=2, link=LINKS["latent"]) as it:
                pairs(LATENT, it, 4)
            add_out()
            norm("mlp1")
            mlp()

            mean(D)
            dve.wait_ge(rstd_ready, c.rstd.at(1))
            c.rstd.now += 1
            g = PC["final1"].start
            for j in range(KT):
                normed(x[:, j, :], params[:, g + j:g + j + 1], x[:, j, :])
            for j in range(KT):
                add_square(j == 0)
            norm("attn2")

            rotate(KTT[:, 0, :], 1.0)
            move(KTT[:, 1, :])
            window = bass.AP(x2[:, :, :].tensor, 0, [x2[:, :, :].ap[0], [2, CMP_M], [S, 2],
                                                     [CMP_STRIDE, CMP_BLOCKS]])
            for kv, pe_name in enumerate(("pe_k", "pe_v")):
                dve.wait_ge(x2_ready, 4 * (kv + 1))
                dve.tensor_tensor(
                    blk[:, :, :].rearrange("p m (g c) -> p m g c", g=2), window,
                    params[:, PC[pe_name]].unsqueeze(2).unsqueeze(3).to_broadcast([P, CMP_M, 2, CMP_BLOCKS]),
                    ALU.add).then_inc(blk_ready, 1)
                dve.wait_ge(blk_hi_ready, kv + 1)
                dve.tensor_tensor(blk_lo[:, :, :], blk[:, :, :], blk_hi[:, :, :].bitcast(F32),
                                  ALU.subtract).then_inc(act_lo, 1)
                c.lo.now += 1
                dve.wait_ge(act_lo, c.lo.at())
                c.gemm.now += 2
                if kv == 0:
                    dst = K_cmp
                else:
                    dst = V_cmpT
                bank = result()
                dve.tensor_copy(dst[0:64, 0:CMP_BLOCKS], bank[0:64, 0:CMP_BLOCKS])
                dve.tensor_copy(dst[64:128, 0:CMP_BLOCKS], bank[0:64, CMP_BLOCKS:CC]).then_inc(gemm_free, 1)
                dve.wait_ge(gemm_free, c.gemm.at())
            move(V_cmp[0:CMP_BLOCKS, :], slice(0, CMP_BLOCKS), slice(0, P))
            for keys, values in ((K_sel, V_sel), (K_win, V_win)):
                rotate(keys[:, :], 1.0)
                move(VT[:, :])
                move(values[:, :, :])
            c.gemm.now += 1
            move(gates[:, :, :], cols=slice(0, NB * 24))
            c.slab.now += 15

            with c.loop(dve, 2, slab=6, gemm=10, step=16, out=2, rope=4, link=LINKS["diff"]) as it:
                project(ROPED, 0, 1, 0, True)
                for par in range(2):
                    attend(STEPS, ROPED if par == 0 else (), 1, roped=True)
                    link(dve.reciprocal(inv[:, 0:8], row_sum[:, par, 0:8]))
                    link(dve.tensor_scalar(inv[:, 4:8], inv[:, 4:8], neg_lam[:, :], None, ALU.mult))
                    y = On[:, par, :, :]
                    t2, t3 = (tmp[:, k, :].rearrange("p (i d) -> p i d", i=NB) for k in (2, 3))
                    dve.tensor_tensor(t2, OB[:, 0, :].rearrange("p (i d) -> p i d", i=NB),
                                      inv[:, 0:4].unsqueeze(2).to_broadcast([P, NB, P]), ALU.mult)
                    link(dve.tensor_tensor(t3, OB[:, 1, :].rearrange("p (i d) -> p i d", i=NB),
                                           inv[:, 4:8].unsqueeze(2).to_broadcast([P, NB, P]), ALU.mult))
                    link(dve.tensor_tensor(t2, t2, t3, ALU.add))
                    link(dve.tensor_tensor(t3, t2, t2, ALU.mult))
                    link(dve.tensor_reduce(small[:, 4:8], t3, X, ALU.add))
                    dve.tensor_scalar(small[:, 4:8], small[:, 4:8], 1.0 / P, EPS, ALU.mult, ALU.add).then_inc(norm2_in, 1)
                    dve.wait_ge(norm2_out, it * 2 + (par + 1))
                    dve.tensor_tensor(y, t2, small[:, 4:8].unsqueeze(2).to_broadcast([P, NB, P]),
                                      ALU.mult).then_inc(o_ready, 1)
                    dve.wait_ge(o_ready, c.out.at(1))
                    tile = it * 2 + par
                    link(dve.tensor_scalar(tmp[:, 2, :], result(), params[:, PC["subln"]], 1.0 - LAM_INIT,
                                           ALU.mult, ALU.mult))
                    link(dve.tensor_scalar(u_hi[:, tile, :], tmp[:, 2, :], 1.0, None, ALU.mult))
                    dve.tensor_tensor(u_lo[:, tile, :], tmp[:, 2, :], u_hi[:, tile, :].bitcast(F32),
                                      ALU.subtract).then_inc(gemm_free, 1)
                    dve.wait_ge(gemm_free, c.gemm.at())
                    c.out.now += 1

            with c.loop(dve, 2, slab=2, gemm=14, step=32, out=2, rope=2, link=LINKS["sparse"]) as it:
                for par in range(2):
                    rotate(QT[:, par, :], QK_SCALE)
                    c.slab.now += 1
                    p3 = pc[:, :, :].rearrange("p (h i) c -> p h i c", h=2)
                    neg, keep = (consts[:, CO[k]].rearrange("p (i c) -> p i c", i=NB)
                                 for k in ("cmp_neg", "cmp_keep"))
                    keep = keep.unsqueeze(1).to_broadcast([P, 2, NB, CMP_BLOCKS])
                    for head in range(2):
                        bank = result(cols=slice(0, NB * CMP_BLOCKS)).rearrange("p (i c) -> p i c", i=NB)
                        dve.tensor_tensor(sc_c[:, NB * head:NB * (head + 1), :], bank, neg,
                                          ALU.add).then_inc(gemm_free, 1)
                    dve.wait_ge(gemm_free, c.gemm.at())
                    link(dve.tensor_reduce(small[:, 8:16], sc_c[:, :, :], X, ALU.max))
                    dve.tensor_tensor(sc_c[:, :, :], sc_c[:, :, :],
                                      small[:, 8:16].unsqueeze(2).to_broadcast([P, 8, CMP_BLOCKS]),
                                      ALU.subtract).then_inc(logits_ready, 1)
                    dve.wait_ge(pc_exp, it * 2 + (par + 1))
                    link(dve.tensor_reduce(small[:, 8:16], pc[:, :, :], X, ALU.add))
                    link(dve.reciprocal(small[:, 16:24], small[:, 8:16]))
                    dve.tensor_tensor(p3, p3, keep, ALU.mult).then_inc(pc_ready, 1)
                    attend([(h, i) for h in range(4) for i in range(NB)])
                    def gate(branch):
                        at = branch * 8 + par
                        pick = gates[:, :, bass.ds(it * 2 + at, 5)]
                        return pick[:, :, ::4].rearrange("p i h -> p h i")
                    link(dve.reciprocal(inv[:, 0:16], row_sum[:, par, 0:16]))
                    w3 = [t.rearrange("p (h i) -> p h i", h=2) for t in (small[:, 16:24], inv[:, 0:8], inv[:, 8:16])]
                    for branch in range(3):
                        last = dve.tensor_tensor(w3[branch], gate(branch), w3[branch], ALU.mult)
                    link(last)
                    dve.tensor_tensor(by_head(tmp[:, 2, :]), by_head(OB[:, 0, :]), over(inv[:, 0:8], HEAD), ALU.mult)
                    link(dve.tensor_tensor(by_head(tmp[:, 3, :]), by_head(OB[:, 1, :]), over(inv[:, 8:16], HEAD),
                                           ALU.mult))
                    link(dve.tensor_tensor(tmp[:, 2, :], tmp[:, 2, :], tmp[:, 3, :], ALU.add))
                    for head in range(2):
                        move(pcT[0:CMP_BLOCKS, head, :], slice(0, CMP_BLOCKS))
                    dve.tensor_tensor(by_head(tmp[:, 3, :]), by_head(result()), over(small[:, 16:24], HEAD),
                                      ALU.mult).then_inc(gemm_free, 1)
                    dve.wait_ge(gemm_free, c.gemm.at())
                    dve.tensor_tensor(flat(par), tmp[:, 2, :], tmp[:, 3, :], ALU.add).then_inc(o_ready, 1)
                    dve.wait_ge(o_ready, c.out.at(1))
                    turned_out(it * 2 + (4 + par))

            with c.loop(dve, 4, slab=6, gemm=8, lo=2, link=LINKS["merge"]) as it:
                for j in range(2):
                    c.gemm.now += 2
                    dve.wait_ge(gemm_free, c.gemm.at())
                    dve.tensor_tensor(tmp[:, 2, :], result(), tmp[:, 0, :], ALU.mult).then_inc(gemm_free, 1)
                    dve.wait_ge(gemm_free, c.gemm.at())
                    dve.tensor_tensor(tmp[:, 3, :], result(), tmp[:, 1, :], ALU.mult).then_inc(gemm_free, 1)
                    dve.wait_ge(gemm_free, c.gemm.at())
                    link(dve.tensor_tensor(tmp[:, 2, :], tmp[:, 2, :], tmp[:, 3, :], ALU.add))
                    n = it * 2 + j
                    link(dve.tensor_scalar(m_hi[:, n, :], tmp[:, 2, :], 1.0, None, ALU.mult))
                    dve.tensor_tensor(m_lo[:, n, :], tmp[:, 2, :], m_hi[:, n, :].bitcast(F32),
                                      ALU.subtract).then_inc(act_lo, 1)
                    c.lo.now += 1
                    dve.wait_ge(act_lo, c.lo.at())
                    c.slab.now += 3
            add_out()
            norm("ffn2")

            def swiglu(tiles):
                for j in range(tiles):
                    s = j % 2
                    c.gemm.now += 1
                    dve.wait_ge(gemm_free, c.gemm.at())
                    dve.tensor_tensor(tmp[:, 2 + s, :], result(), tmp[:, s, :], ALU.mult).then_inc(gemm_free, 1)
                    dve.wait_ge(gemm_free, c.gemm.at())
                    c.slab.now += 2
                    split_u(j, s)
                add_out()
                c.slab.now += 8

            with c.loop(dve, 2, slab=24, gemm=24, hi=8, lo=8, acc=8):
                swiglu(8)
            swiglu(FF2_TILES - 16)
            mean(D)
            dve.wait_ge(rstd_ready, c.rstd.at(1))
            g = PC["final2"].start
            for j in range(KT):
                normed(x[:, j, :], params[:, g + j:g + j + 1], x[:, j, :])


LINKS = {"fox": 4, "chunked": 4, "stick": 34, "latent": 8, "diff": 20, "sparse": 18, "merge": 4}


def tiles_of(w):
    return w.reshape(-1, P, w.shape[1]).transpose(1, 0, 2)


def slab(w):
    out = np.zeros((P, 8, P), np.float32)
    t = tiles_of(w)
    out[:, :t.shape[1], :t.shape[2]] = t
    return out.reshape(P, SLAB)


def pack_slabs(a):
    def column_tiles(w, n=None):
        return [slab(w[:, j:j + P]) for j in range(0, w.shape[1], P)]

    def heads(w, at):
        return [slab(w[:, at + 512 * part + P * p:at + 512 * part + P * (p + 1)])
                for p in range(4) for part in (2, 0, 1)]

    def down(w, rows):
        return column_tiles(w[rows])

    def mlp(layer):
        out = []
        for q in range(4):
            f = slice(q * 1024, (q + 1) * 1024)
            out += column_tiles(a["w_up"][layer][:, f]) + down(a["w_down"][layer], f)
        return out

    out = []
    w = a["w_in_ab"][0]
    out.append(slab(w[:, 1536:1544]))
    out += heads(w, 0) + heads(w, 1544)
    out += column_tiles(a["w_out_ab"][0]) + mlp(0)

    w = a["w_in_cd"][0]
    cq, ckv, kr = w[:, 1536:1920], w[:, 1920:2176], w[:, 2176:2208]
    out += column_tiles(cq) + [slab(np.concatenate([kr, kr[:, 16:], kr[:, :16]], 1))] + column_tiles(ckv)
    out += heads(w, 0)
    for h in range(8):
        uq, ukv = a["w_uq"][0][:, 96 * h:96 * h + 96], a["w_ukv"][0][:, P * h:P * (h + 1)]
        s = slab(np.concatenate([uq, uq[:, 80:96], uq[:, 64:80]], 1)).reshape(P, 8, P)
        s[:, Q_TILES:C_TILES] = tiles_of(ukv)
        out.append(s.reshape(P, SLAB))
    out += column_tiles(a["w_out_cd"][0]) + mlp(1)

    w = a["w_in_2"][0]
    kv = [w[:, 2048 + P * j:2048 + P * (j + 1)] for j in range(6)]
    out += [slab(kv[0]), slab(kv[1])]
    for name in ("cmp_k_w1_2", "cmp_v_w1_2"):
        t = tiles_of(a[name][0])
        out += [np.ascontiguousarray(t[:, 4 * q:4 * q + 4]).reshape(P, SLAB) for q in range(4)]
    out += [slab(k) for k in kv[2:]]
    out.append(slab(w[:, 2816:2840]))
    for h in range(4):
        out += [slab(w[:, 512 * part + P * h:512 * part + P * (h + 1)]) for part in range(3)]
    pair_cols = [np.r_[64 * h:64 * h + 64, 64 * (h + 4):64 * (h + 4) + 64] for h in range(4)]
    out += [slab(w[:, 1536 + cols]) for cols in pair_cols]
    w_b = a["w_branch_b_2"][0][np.concatenate(pair_cols)]
    for n in range(KT):
        cols = slice(n * P, (n + 1) * P)
        out += [slab(w[:, 2840:3864][:, cols]), slab(w[:, 3864:4888][:, cols]),
                slab(np.concatenate([a["w_branch_a_2"][0][:, cols], w_b[:, cols]], 0))]
    out += column_tiles(a["w_out_2"][0])
    for first, tiles in ((0, 8), (8, 8), (16, 6)):
        for j in range(first, first + tiles):
            f = slice(j * P, (j + 1) * P)
            out += [slab(a["w_gate_2"][0][:, f]), slab(a["w_up_2"][0][:, f])]
        out += down(a["w_down_2"][0], slice(first * P, (first + tiles) * P))
    out += [np.zeros((P, SLAB), np.float32)] * (2 + len(out) % 2)
    return np.stack(out)


def pack_params(a):
    def col(v):
        return v.reshape(-1, P).T
    out = np.zeros((P, N_PARAM), np.float32)
    for name, v in (("mix0", a["norm_mix"][0]), ("mlp0", a["norm_mlp"][0]), ("mix1", a["norm_mix"][1]),
                    ("mlp1", a["norm_mlp"][1]), ("final1", a["norm_final"]), ("q_norm", a["q_norm"][0]),
                    ("kv_norm", a["kv_norm"][0]), ("attn2", a["attn_norm_g_2"][0]),
                    ("ffn2", a["ffn_norm_g_2"][0]), ("final2", a["final_norm_g_2"]),
                    ("subln", a["diff_subln_g_2"][0]), ("pe_k", a["cmp_pe_k_2"][0]),
                    ("pe_v", a["cmp_pe_v_2"][0])):
        out[:, PC[name]] = col(v.reshape(-1))
    out[0:8, PC["b_forget"]] = a["b_forget"][0][:, None]
    for name, key in (("w2_k", "cmp_k_w2_2"), ("w2_v", "cmp_v_w2_2")):
        out[:, PC[name]] = tiles_of(a[key][0]).reshape(P, 128)
    return out


def pack_consts():
    p, f = np.arange(P)[:, None], np.arange(P)[None, :]
    out = np.zeros((P, N_CONST), np.float32)
    out[:, CO["ident"]] = p == f
    out[:, CO["anti"]] = p + f == P - 1
    out[:, CO["causal"]] = np.where(f <= p, 0, NEG)
    out[:, CO["strict"]] = np.where(f < p, 0, NEG)
    out[:, CO["chunk"]] = np.where(f // CHUNK <= p // CHUNK, 0, NEG)
    out[:, CO["ones"]] = 1
    out[:, CO["onehot"]] = p % 32 == np.arange(8)[None, :]
    theta = np.float32(10000.0)
    half = np.arange(16, dtype=np.float32)
    freq1 = theta ** (-half / np.float32(16))
    freq2 = np.float32(1) / theta ** (np.arange(0, 64, 2, dtype=np.float32) / np.float32(64))
    q = np.arange(P)
    out[:, CO["freq1"]] = freq1[q % 16][:, None]
    out[:, CO["sign1"]] = np.where(q % 32 < 16, -1, 1)[:, None]
    out[:, CO["freq2"]] = freq2[q % 32][:, None]
    out[:, CO["sign2"]] = np.where(q % 64 < 32, -1, 1)[:, None]
    out[:, CO["half_pi"]] = np.pi / 2
    ends = np.arange(CMP_BLOCKS) * CMP_STRIDE + CMP_LEN - 1
    seen = ends[None, None, :] <= (np.arange(NB)[None, :, None] * P + q[:, None, None])
    out[:, CO["cmp_neg"]] = np.where(seen, 0, NEG).reshape(P, -1)
    out[:, CO["cmp_keep"]] = seen.reshape(P, -1)
    return out


def kernel(**inputs):
    import concourse.bacc as bacc
    from concourse.bass_utils import run_bass_kernel_spmd as run

    a = {name: np.asarray(v) for name, v in inputs.items()}
    arrays = {
        "slabs": pack_slabs(a),
        "x_t": np.ascontiguousarray(a["x"][0].T),
        "params_packed": pack_params(a),
        "consts_packed": pack_consts(),
        "pos1": a["positions"].reshape(S),
        "pos2": a["positions_2"].reshape(S),
        "rel": np.ascontiguousarray(a["rel_bias"][0]),
        "lam": a["diff_lambda_2"].reshape(4 * HEAD),
    }
    nc = bacc.Bacc("TRN2", target_bir_lowering=False, num_devices=1)
    args = [nc.dram_tensor(name, v.shape, mybir.dt.from_np(v.dtype), kind="ExternalInput").ap()
            for name, v in arrays.items()]
    y = nc.dram_tensor("y_t", (D, S), F32, kind="ExternalOutput").ap()
    build(nc, *args, y)
    r = run(nc, [arrays], core_ids=[0])
    return np.ascontiguousarray(r.results[0]["y_t"].T)[None]
```
